# Optimizing a Trainium2 kernel written in Bass

```python
import math
import jax, jax.numpy as jnp
from jax import lax
import numpy as np

D_MODEL = 1024
BATCH = 1
SEQ = 256
DEPTH = 2

N_MIXERS = 4
ROPE_THETA = 500000.0
NORM_EPS = 1e-6
QBLK = 128
NEG_INF = -1e30
POS_BIG = 1e30
D_FF = ((-(-8 * D_MODEL // 3) + 255) // 256) * 256

NSA_HEAD_DIM = 64
NSA_HEADS = D_MODEL // NSA_HEAD_DIM
NSA_KV_HEADS = 4
CMP_LEN = 32
CMP_STRIDE = 16
CMP_HIDDEN = 4 * NSA_HEAD_DIM
SEL_LEN = 64
SEL_TOP = 16
NSA_WIN = 512

MLA_HEADS = 16
MLA_NOPE = 64
MLA_ROPE = 32
MLA_V = 64
MLA_Q_LORA = 768
MLA_KV_LORA = 256

SWA_HEADS = 16
SWA_KV_HEADS = 2
SWA_HEAD_DIM = 64
SWA_WIN = 128

DIFF_HEAD_DIM = 64
DIFF_HEADS = D_MODEL // (2 * DIFF_HEAD_DIM)

kernel_name = "hybrid_nsa_mla_swa_diff_interleaved"

def rms_norm(x, g):
    xf = x.astype(jnp.float32)
    y = xf * lax.rsqrt(jnp.mean(xf * xf, axis=-1, keepdims=True) + NORM_EPS)
    return (y * g.astype(jnp.float32)).astype(x.dtype)

def rope(x, pos, rot_dim):
    half = rot_dim // 2
    inv_freq = ROPE_THETA ** (-jnp.arange(half, dtype=jnp.float32) / half)
    ang = pos.astype(jnp.float32)[:, :, None] * inv_freq
    cos = jnp.cos(ang)[:, :, None, :]
    sin = jnp.sin(ang)[:, :, None, :]
    xf = x.astype(jnp.float32)
    x1, x2, rest = xf[..., :half], xf[..., half:rot_dim], xf[..., rot_dim:]
    return jnp.concatenate([x1 * cos - x2 * sin, x2 * cos + x1 * sin, rest], axis=-1).astype(x.dtype)

def masked_softmax(s, valid):
    return jax.nn.softmax(jnp.where(valid, s.astype(jnp.float32), NEG_INF), axis=-1)

def sweep_query_blocks(block_fn, seq):
    out = lax.map(block_fn, jnp.arange(seq // QBLK))
    b = out.shape[1]
    return jnp.swapaxes(out, 0, 1).reshape(b, seq, out.shape[-1])

def swiglu(h, w_gate, w_up, w_down):
    return (jax.nn.silu(h @ w_gate) * (h @ w_up)) @ w_down

def compress_blocks(t, pe, w1, w2):
    B, S, G, hd = t.shape
    ch = t.reshape(B, S // CMP_STRIDE, CMP_STRIDE, G, hd)
    blk = jnp.concatenate([ch[:, :-1], ch[:, 1:]], axis=2) + pe[:, None, :]
    blk = jnp.moveaxis(blk, 3, 2).reshape(B, -1, G, CMP_LEN * hd)
    return jax.nn.gelu(blk @ w1) @ w2

def nsa_mixer(h, pos, w_in, cmp_pe_k, cmp_w1_k, cmp_w2_k, cmp_pe_v, cmp_w1_v, cmp_w2_v, w_out):
    B, S, _ = h.shape
    H, G, hd = NSA_HEADS, NSA_KV_HEADS, NSA_HEAD_DIM
    hpg = H // G
    n_cmp = S // CMP_STRIDE - 1
    n_sel = S // SEL_LEN
    n_top = min(SEL_TOP, n_sel)
    scale = hd ** -0.5
    rot = hd // 4
    kvw = G * hd
    cuts = [H * hd + j * kvw for j in range(7)]
    q, kc, vc, ks, vs, kw, vw, g = jnp.split(h @ w_in, cuts, axis=-1)
    q = rope(q.reshape(B, S, H, hd), pos, rot)
    kc, vc, ks, vs, kw, vw = (t.reshape(B, S, G, hd) for t in (kc, vc, ks, vs, kw, vw))
    ks = rope(ks, pos, rot)
    kw = rope(kw, pos, rot)
    gates = jax.nn.sigmoid(g.astype(jnp.float32)).reshape(B, S, G, hpg, 3)
    pos_cmp = pos.reshape(B, S // CMP_STRIDE, CMP_STRIDE)[:, 1:, -1]
    k_cmp = rope(compress_blocks(kc, cmp_pe_k, cmp_w1_k, cmp_w2_k), pos_cmp, rot)
    v_cmp = compress_blocks(vc, cmp_pe_v, cmp_w1_v, cmp_w2_v)
    k_selb = jnp.moveaxis(ks.reshape(B, n_sel, SEL_LEN, G, hd), 3, 1)
    v_selb = jnp.moveaxis(vs.reshape(B, n_sel, SEL_LEN, G, hd), 3, 1)
    padw = ((0, 0), (NSA_WIN, 0), (0, 0), (0, 0))
    k_winp = jnp.pad(kw, padw)
    v_winp = jnp.pad(vw, padw)
    cmp_idx = jnp.arange(n_cmp)
    sel_idx = jnp.arange(n_sel)
    cmp_end = cmp_idx * CMP_STRIDE + CMP_LEN - 1
    sel_start = sel_idx * SEL_LEN
    cover = ((cmp_idx[:, None] * CMP_STRIDE <= sel_start[None, :] + SEL_LEN - 1)
             & (cmp_end[:, None] >= sel_start[None, :])).astype(jnp.float32)
    b_ix = jnp.arange(B)[:, None, None, None]
    g_ix = jnp.arange(G)[None, :, None, None]

    def block(c):
        q0 = c * QBLK
        qi = q0 + jnp.arange(QBLK)
        qb = lax.dynamic_slice_in_dim(q, q0, QBLK, 1).reshape(B, QBLK, G, hpg, hd)
        s = jnp.einsum('bqghd,bngd->bghqn', qb, k_cmp) * scale
        valid = cmp_end[None, :] <= qi[:, None]
        p = masked_softmax(s, valid) * valid
        o_cmp = jnp.einsum('bghqn,bngd->bqghd', p.astype(v_cmp.dtype), v_cmp)
        imp = jnp.einsum('bghqn,nj->bgqj', p, cover)
        forced = (sel_idx[None, :] == (qi // SEL_LEN)[:, None]) | (sel_idx[None, :] == 0)
        imp = jnp.where(forced, POS_BIG, imp)
        imp = jnp.where(sel_start[None, :] <= qi[:, None], imp, NEG_INF)
        _, top = lax.top_k(imp, n_top)
        k_g = k_selb[b_ix, g_ix, top].reshape(B, G, QBLK, n_top * SEL_LEN, hd)
        v_g = v_selb[b_ix, g_ix, top].reshape(B, G, QBLK, n_top * SEL_LEN, hd)
        tok = (top[..., None] * SEL_LEN + jnp.arange(SEL_LEN)).reshape(B, G, QBLK, n_top * SEL_LEN)
        s = jnp.einsum('bqghd,bgqkd->bghqk', qb, k_g) * scale
        valid = (tok <= qi[None, None, :, None])[:, :, None]
        p = masked_softmax(s, valid)
        o_sel = jnp.einsum('bghqk,bgqkd->bqghd', p.astype(v_g.dtype), v_g)
        k_w = lax.dynamic_slice_in_dim(k_winp, q0, QBLK + NSA_WIN, 1)
        v_w = lax.dynamic_slice_in_dim(v_winp, q0, QBLK + NSA_WIN, 1)
        ki = q0 - NSA_WIN + jnp.arange(QBLK + NSA_WIN)
        valid = (ki[None, :] >= 0) & (ki[None, :] <= qi[:, None]) & (ki[None, :] > qi[:, None] - NSA_WIN)
        s = jnp.einsum('bqghd,bkgd->bghqk', qb, k_w) * scale
        p = masked_softmax(s, valid)
        o_win = jnp.einsum('bghqk,bkgd->bqghd', p.astype(v_w.dtype), v_w)
        gb = lax.dynamic_slice_in_dim(gates, q0, QBLK, 1)
        o = gb[..., 0:1] * o_cmp + gb[..., 1:2] * o_sel + gb[..., 2:3] * o_win
        return o.reshape(B, QBLK, H * hd).astype(h.dtype)

    return sweep_query_blocks(block, S) @ w_out

def mla_mixer(h, pos, w_in, q_norm_g, kv_norm_g, w_q_up, w_kv_up, w_out):
    B, S, _ = h.shape
    H = MLA_HEADS
    dk = MLA_NOPE + MLA_ROPE
    q_lat, kv_lat, k_pe = jnp.split(h @ w_in, [MLA_Q_LORA, MLA_Q_LORA + MLA_KV_LORA], axis=-1)
    q = (rms_norm(q_lat, q_norm_g) @ w_q_up).reshape(B, S, H, dk)
    q = jnp.concatenate([q[..., :MLA_NOPE], rope(q[..., MLA_NOPE:], pos, MLA_ROPE)], axis=-1)
    kv = (rms_norm(kv_lat, kv_norm_g) @ w_kv_up).reshape(B, S, H, MLA_NOPE + MLA_V)
    k_pe = rope(k_pe[:, :, None, :], pos, MLA_ROPE)
    k = jnp.concatenate([kv[..., :MLA_NOPE], jnp.broadcast_to(k_pe, (B, S, H, MLA_ROPE))], axis=-1)
    v = kv[..., MLA_NOPE:]
    scale = dk ** -0.5
    kidx = jnp.arange(S)

    def block(c):
        q0 = c * QBLK
        qi = q0 + jnp.arange(QBLK)
        qb = lax.dynamic_slice_in_dim(q, q0, QBLK, 1)
        s = jnp.einsum('bqhd,bkhd->bhqk', qb, k) * scale
        p = masked_softmax(s, kidx[None, :] <= qi[:, None])
        o = jnp.einsum('bhqk,bkhd->bqhd', p.astype(v.dtype), v)
        return o.reshape(B, QBLK, H * MLA_V)

    return sweep_query_blocks(block, S) @ w_out

def swa_sink_mixer(h, pos, w_in, sinks, w_out):
    B, S, _ = h.shape
    H, G, hd, W = SWA_HEADS, SWA_KV_HEADS, SWA_HEAD_DIM, SWA_WIN
    hpg = H // G
    nb = S // W
    rot = hd // 4
    q, k, v = jnp.split(h @ w_in, [H * hd, H * hd + G * hd], axis=-1)
    q = rope(q.reshape(B, S, H, hd), pos, rot).reshape(B, nb, W, G, hpg, hd)
    k = rope(k.reshape(B, S, G, hd), pos, rot).reshape(B, nb, W, G, hd)
    v = v.reshape(B, nb, W, G, hd)

    def with_prev(t):
        prev = jnp.pad(t, ((0, 0), (1, 0), (0, 0), (0, 0), (0, 0)))[:, :-1]
        return jnp.concatenate([prev, t], axis=2)

    kk, vv = with_prev(k), with_prev(v)
    s = jnp.einsum('bnqghd,bnkgd->bnghqk', q, kk) * hd ** -0.5
    qi = jnp.arange(W)[:, None] + W
    ki = jnp.arange(2 * W)[None, :]
    band = (ki <= qi) & (ki > qi - W)
    real = (jnp.arange(nb)[:, None, None] > 0) | (ki >= W)[None]
    valid = (band[None] & real)[None, :, None, None]
    s = jnp.where(valid, s.astype(jnp.float32), NEG_INF)
    sink = jnp.broadcast_to(sinks.astype(jnp.float32).reshape(1, 1, G, hpg, 1, 1), s.shape[:-1] + (1,))
    p = jax.nn.softmax(jnp.concatenate([s, sink], axis=-1), axis=-1)[..., :-1]
    o = jnp.einsum('bnghqk,bnkgd->bnqghd', p.astype(vv.dtype), vv)
    return o.reshape(B, S, H * hd) @ w_out

def diff_mixer(h, pos, w_in, lam_q1, lam_k1, lam_q2, lam_k2, subln_g, w_out, lam_init):
    B, S, _ = h.shape
    H, d = DIFF_HEADS, DIFF_HEAD_DIM
    rot = d // 4
    q, k, v = jnp.split(h @ w_in, [H * 2 * d, 2 * H * 2 * d], axis=-1)
    q = q.reshape(B, S, H, 2, d)
    k = k.reshape(B, S, H, 2, d)
    q1, q2 = rope(q[..., 0, :], pos, rot), rope(q[..., 1, :], pos, rot)
    k1, k2 = rope(k[..., 0, :], pos, rot), rope(k[..., 1, :], pos, rot)
    v = v.reshape(B, S, H, 2 * d)
    lam = (jnp.exp(jnp.sum(lam_q1.astype(jnp.float32) * lam_k1.astype(jnp.float32)))
           - jnp.exp(jnp.sum(lam_q2.astype(jnp.float32) * lam_k2.astype(jnp.float32))) + lam_init)
    scale = d ** -0.5
    kidx = jnp.arange(S)

    def block(c):
        q0 = c * QBLK
        qi = q0 + jnp.arange(QBLK)
        causal = kidx[None, :] <= qi[:, None]
        p1 = masked_softmax(jnp.einsum('bqhd,bkhd->bhqk', lax.dynamic_slice_in_dim(q1, q0, QBLK, 1), k1) * scale, causal)
        p2 = masked_softmax(jnp.einsum('bqhd,bkhd->bhqk', lax.dynamic_slice_in_dim(q2, q0, QBLK, 1), k2) * scale, causal)
        o = jnp.einsum('bhqk,bkhd->bqhd', (p1 - lam * p2).astype(v.dtype), v)
        return o.reshape(B, QBLK, H * 2 * d)

    o = sweep_query_blocks(block, S).reshape(B, S, H, 2 * d)
    o = rms_norm(o, subln_g) * (1.0 - lam_init)
    return o.reshape(B, S, H * 2 * d) @ w_out

def setup_inputs(seed: int = 0) -> dict:
    key = jax.random.key(seed)
    keys = iter(jax.random.split(key, 48))

    def nrm(shape, scale):
        return scale * jax.random.normal(next(keys), shape, jnp.float32)

    def lin(shape):
        return nrm(shape, shape[-2] ** -0.5)

    def gain(shape):
        return 1.0 + nrm(shape, 0.1)

    L, D, F = DEPTH, D_MODEL, D_FF
    n_nsa, n_mla, n_swa, n_diff = (len(range(m, DEPTH, N_MIXERS)) for m in range(N_MIXERS))
    nsa_in = NSA_HEADS * NSA_HEAD_DIM + 6 * NSA_KV_HEADS * NSA_HEAD_DIM + 3 * NSA_HEADS
    x = jax.random.normal(next(keys), (BATCH, SEQ, D), jnp.float32)
    positions = jnp.broadcast_to(jnp.arange(SEQ, dtype=jnp.int32)[None, :], (BATCH, SEQ))
    return {
        "x": x,
        "positions": positions,
        "ln_mix_pre": gain((L, D)),
        "ln_mix_post": gain((L, D)),
        "ln_ffn_pre": gain((L, D)),
        "ln_ffn_post": gain((L, D)),
        "ffn_w_gate": lin((L, D, F)),
        "ffn_w_up": lin((L, D, F)),
        "ffn_w_down": lin((L, F, D)),
        "nsa_w_in": lin((n_nsa, D, nsa_in)),
        "nsa_cmp_pe_k": nrm((n_nsa, CMP_LEN, NSA_HEAD_DIM), 0.1),
        "nsa_cmp_w1_k": lin((n_nsa, CMP_LEN * NSA_HEAD_DIM, CMP_HIDDEN)),
        "nsa_cmp_w2_k": lin((n_nsa, CMP_HIDDEN, NSA_HEAD_DIM)),
        "nsa_cmp_pe_v": nrm((n_nsa, CMP_LEN, NSA_HEAD_DIM), 0.1),
        "nsa_cmp_w1_v": lin((n_nsa, CMP_LEN * NSA_HEAD_DIM, CMP_HIDDEN)),
        "nsa_cmp_w2_v": lin((n_nsa, CMP_HIDDEN, NSA_HEAD_DIM)),
        "nsa_w_out": lin((n_nsa, NSA_HEADS * NSA_HEAD_DIM, D)),
        "mla_w_in": lin((n_mla, D, MLA_Q_LORA + MLA_KV_LORA + MLA_ROPE)),
        "mla_q_norm": gain((n_mla, MLA_Q_LORA)),
        "mla_kv_norm": gain((n_mla, MLA_KV_LORA)),
        "mla_w_q_up": lin((n_mla, MLA_Q_LORA, MLA_HEADS * (MLA_NOPE + MLA_ROPE))),
        "mla_w_kv_up": lin((n_mla, MLA_KV_LORA, MLA_HEADS * (MLA_NOPE + MLA_V))),
        "mla_w_out": lin((n_mla, MLA_HEADS * MLA_V, D)),
        "swa_w_in": lin((n_swa, D, (SWA_HEADS + 2 * SWA_KV_HEADS) * SWA_HEAD_DIM)),
        "swa_sinks": nrm((n_swa, SWA_HEADS), 0.5),
        "swa_w_out": lin((n_swa, SWA_HEADS * SWA_HEAD_DIM, D)),
        "diff_w_in": lin((n_diff, D, 3 * DIFF_HEADS * 2 * DIFF_HEAD_DIM)),
        "diff_lam_q1": nrm((n_diff, DIFF_HEAD_DIM), 0.1),
        "diff_lam_k1": nrm((n_diff, DIFF_HEAD_DIM), 0.1),
        "diff_lam_q2": nrm((n_diff, DIFF_HEAD_DIM), 0.1),
        "diff_lam_k2": nrm((n_diff, DIFF_HEAD_DIM), 0.1),
        "diff_subln": gain((n_diff, 2 * DIFF_HEAD_DIM)),
        "diff_w_out": lin((n_diff, DIFF_HEADS * 2 * DIFF_HEAD_DIM, D)),
    }

def reference(x, positions, ln_mix_pre, ln_mix_post, ln_ffn_pre, ln_ffn_post, ffn_w_gate, ffn_w_up, ffn_w_down,
              nsa_w_in, nsa_cmp_pe_k, nsa_cmp_w1_k, nsa_cmp_w2_k, nsa_cmp_pe_v, nsa_cmp_w1_v, nsa_cmp_w2_v, nsa_w_out,
              mla_w_in, mla_q_norm, mla_kv_norm, mla_w_q_up, mla_w_kv_up, mla_w_out,
              swa_w_in, swa_sinks, swa_w_out,
              diff_w_in, diff_lam_q1, diff_lam_k1, diff_lam_q2, diff_lam_k2, diff_subln, diff_w_out):
    h = x
    for i in range(DEPTH):
        kind, j = i % N_MIXERS, i // N_MIXERS
        u = rms_norm(h, ln_mix_pre[i])
        if kind == 0:
            m = nsa_mixer(u, positions, nsa_w_in[j], nsa_cmp_pe_k[j], nsa_cmp_w1_k[j], nsa_cmp_w2_k[j],
                          nsa_cmp_pe_v[j], nsa_cmp_w1_v[j], nsa_cmp_w2_v[j], nsa_w_out[j])
        elif kind == 1:
            m = mla_mixer(u, positions, mla_w_in[j], mla_q_norm[j], mla_kv_norm[j], mla_w_q_up[j],
                          mla_w_kv_up[j], mla_w_out[j])
        elif kind == 2:
            m = swa_sink_mixer(u, positions, swa_w_in[j], swa_sinks[j], swa_w_out[j])
        else:
            lam_init = 0.8 - 0.6 * math.exp(-0.3 * i)
            m = diff_mixer(u, positions, diff_w_in[j], diff_lam_q1[j], diff_lam_k1[j], diff_lam_q2[j],
                           diff_lam_k2[j], diff_subln[j], diff_w_out[j], lam_init)
        h = h + rms_norm(m, ln_mix_post[i])
        u = rms_norm(h, ln_ffn_pre[i])
        h = h + rms_norm(swiglu(u, ffn_w_gate[i], ffn_w_up[i], ffn_w_down[i]), ln_ffn_post[i])
    return h


_drawn_inputs = setup_inputs


def setup_inputs(seed=0):
    import zlib

    import numpy as np

    out = dict(_drawn_inputs(seed))
    spreads = {}
    factors = {'nsa_cmp_pe_k': 3.005}
    for name, (base, spread) in spreads.items():
        noise = np.random.default_rng([zlib.crc32(name.encode()), seed]).standard_normal(out[name].shape)
        drawn = base * np.exp(spread * noise) if base else spread * noise
        out[name] = __import__('jax').numpy.asarray(drawn.astype(out[name].dtype))
    for name, factor in factors.items():
        out[name] = (out[name] * factor).astype(out[name].dtype)
    return out
```

```python
import math
from contextlib import ExitStack

import concourse.bass as bass
from concourse import mybir
from concourse.alu_op_type import AluOpType as ALU

F32 = mybir.dt.float32
F32R = mybir.dt.float32r
I32 = mybir.dt.int32
ACT = mybir.ActivationFunctionType
AX = mybir.AxisListType

P = 128
SEQ, D, F = 256, 1024, 2816
T = SEQ // P
KC = D // P
EPS = 1e-6
NEG = -1e30
HD = 64
HEADS = 16
QUAD = 4
TURNS = HEADS // QUAD
UNITS = T * QUAD
KVW = 256
CMP_STRIDE, CMP_LEN = 16, 32
NCMP = SEQ // CMP_STRIDE - 1
CROWS = QUAD * NCMP
CK = CMP_LEN * HD // P
GATES = 3 * HEADS
NOPE, ROPE = 64, 32
DK = NOPE + ROPE
QLAT, KVLAT = 768, 256
QC, KVC = QLAT // P, KVLAT // P
FB = 256
STEPS = F // FB
SLOT = 2048
NSA_LINKS, MLA_LINKS = 29, 15

SEL_SCALE = HD ** -0.5
MLA_SCALE = DK ** -0.5
TWO_PI = 2 * math.pi
ROUND = 1.5 * 2.0 ** 23


def two_pi_parts():
    parts, rest = [], TWO_PI
    for _ in range(3):
        unit = 2.0 ** (math.floor(math.log2(rest)) - 7)
        part = math.floor(rest / unit) * unit
        parts.append(part)
        rest -= part
    return parts + [rest]


NSA_KV = 0
NSA_GATES = NSA_KV + 6
NSA_W1K = NSA_GATES + 1
NSA_Q0 = NSA_W1K + 2
NSA_W1V = NSA_Q0 + 3
NSA_Q1 = NSA_W1V + 2
NSA_OUT = NSA_Q1 + 3 * (TURNS - 1)
FFN0 = NSA_OUT + 4
MLA_IN = FFN0 + 3 * STEPS
MLA_UP0 = MLA_IN + 5
MLA_UP1 = MLA_UP0 + 3
MLA_OUT = MLA_UP1 + 3 * (TURNS - 1)
FFN1 = MLA_OUT + 4
TILES = FFN1 + 3 * STEPS


class Tally:

    def __init__(self, eng, sem):
        self.eng, self.sem, self.n, self.turn, self.per = eng, sem, 0, None, 0

    def link(self, ins):
        ins.then_inc(self.sem, 1)
        self.n += 1
        self.eng.wait_ge(self.sem, self.n if self.turn is None else self.turn * self.per + self.n)

    def enter(self, turn, per):
        self.turn, self.per, self.at = turn, per, self.n

    def leave(self, turns):
        assert self.n - self.at == self.per, (self.n - self.at, self.per)
        self.turn, self.n = None, self.at + self.per * turns


def trunk(nc, x, positions, inv_freq, gains, lat_gain, nsa_w_in, pe_k, pe_v, w1_k, w1_v, w2_k, w2_v, nsa_w_out,
          mla_w_in, w_q_up, w_kv_up, mla_w_out, w_gate_up, w_down, out):
    with ExitStack() as ctx:
        def sb(name, shape, dt=F32):
            return ctx.enter_context(nc.sbuf_tensor(name, shape, dt))

        sems = {}

        def sem(name):
            if name not in sems:
                sems[name] = ctx.enter_context(nc.semaphore(name))
            return sems[name]

        raw = [sb(f"raw{i}", [P, SLOT]) for i in range(3)]
        w_hi = [sb(f"w_hi{i}", [P, SLOT], F32R) for i in range(3)]
        w_lo = [sb(f"w_lo{i}", [P, SLOT], F32R) for i in range(3)]
        act_hi = sb("act_hi", [P, KC, SEQ], F32R)
        act_lo = sb("act_lo", [P, KC, SEQ], F32R)
        h = sb("h", [P, T, D])
        u = sb("u", [P, T, D])
        gain = sb("gain", [P, 4, D])
        stats = sb("stats", [P, 64])
        ident = sb("ident", [P, P])
        mask = sb("mask", [P, SEQ])
        zero = sb("zero", [P, 512], F32R)
        cos = sb("cos", [P, T + 1, 16])
        sin = sb("sin", [P, T + 1, 16])
        rope_tmp = sb("rope_tmp", [P, 4, 128])
        hidT_hi = sb("hidT_hi", [P, 2, SEQ], F32R)
        hidT_lo = sb("hidT_lo", [P, 2, SEQ], F32R)
        qs = sb("qs", [P, T, QUAD * DK])
        qT = sb("qT", [P, QUAD, SEQ])
        s_sb = sb("s_sb", [P, 2, 512])
        pT = sb("pT", [P, 2, 512])
        silu = pT[:, 0, :].rearrange("p (t n) -> p t n", t=T)
        hid = pT[:, 1, :].rearrange("p (t n) -> p t n", t=T)
        smax = sb("smax", [P, 2, 2])
        nmax = sb("nmax", [P, 2, 2])
        waited = sb("waited", [P, 1])
        rsum = sb("rsum", [P, T, QUAD, 3])
        fac = sb("fac", [P, T, QUAD, 3])
        lat_g = sb("lat_g", [P, D])
        o_tmp = lat_g[:, 0:3 * KVW].rearrange("p (b n) -> p b n", b=3)
        big = sb("big", [P, 12288])

        def carve(sizes):
            at, parts = 0, []
            for n in sizes:
                parts.append(big[:, at:at + n])
                at += n
            assert at <= 12288, at
            return parts

        kvc_, ks_, kT_, vs_, kc2_, vc2_, blkf_, w2_, vbd_, cs_, hidc_, hidcT_, small_ = carve(
            [T * 1024, T * 512, QUAD * 512, T * 512, 4 * SEQ, 4 * SEQ, CK * CROWS, 2 * 2 * HD, TURNS * KVW, T * 64,
             2 * 256, 2 * CROWS + 2 * TURNS * CROWS, 448])
        kvc = kvc_.rearrange("p (t n) -> p t n", t=T)
        kstage = ks_.rearrange("p (t n) -> p t n", t=T)
        kT = kT_.rearrange("p (g n) -> p g n", g=QUAD)
        vsw = vs_.rearrange("p (t b n) -> p t b n", t=T, b=2)
        c2T = [a.rearrange("p (g s) -> p g s", g=4) for a in (kc2_, vc2_)]
        blkf = blkf_
        w2 = w2_.rearrange("p (v c n) -> p v c n", v=2, c=2)
        vbd = vbd_.rearrange("p (g n) -> p g n", g=TURNS)
        cs = cs_.rearrange("p (t n) -> p t n", t=T)
        hidc = hidc_.rearrange("p (v n) -> p v n", v=2)
        hidcT = hidcT_[:, 0:2 * CROWS].rearrange("p (c n) -> p c n", c=2)
        hidcT_rep = hidcT_[:, 2 * CROWS:].rearrange("p (c g i n) -> p c g i n", c=2, g=TURNS, i=QUAD)
        kcs, kcT, cT = small_[:, 0:64], small_[:, 64:124], small_[:, 128:256]
        gates = small_[:, 256:256 + T * GATES].rearrange("p (t n) -> p t n", t=T)
        peT = small_[:, 352:384].rearrange("p (v c) -> p v c", v=2)
        cmax = small_[:, 384:388]
        blk_hi = sb("blk_hi", [P, CK, CROWS], F32R)
        blk_lo = sb("blk_lo", [P, CK, CROWS], F32R)
        cmask = sb("cmask", [P, T, NCMP])
        anyvalid = sb("anyvalid", [P, T])
        blockmask = sb("blockmask", [P, QUAD])
        lat_, mk_, mkT_, mv_ = carve([T * (D + ROPE), T * QUAD * DK, QUAD * SEQ, T * HEADS * HD])
        lat = lat_.rearrange("p (t n) -> p t n", t=T)
        mk = mk_.rearrange("p (t i n) -> p t i n", t=T, i=QUAD)
        mkT = mkT_.rearrange("p (i s) -> p i s", i=QUAD)
        mv = mv_.rearrange("p (t n) -> p t n", t=T)
        pos_i = sb("pos_i", [P, T + 1], I32)
        pos_f = sb("pos_f", [P, T + 1])
        invf = sb("invf", [P, 16])
        ang = sb("ang", [P, 3, (T + 1) * 16])
        lstats = sb("lstats", [P, 8])

        bank = [ctx.enter_context(nc.psum_tensor(f"bank{i}", [P, 512], F32)) for i in range(8)]

        def rows(w, c0, n, cols):
            return w[c0 * P:(c0 + n) * P, cols].rearrange("(c p) n -> p c n", p=P)

        loaded = [sem(f"slot{i}_loaded") for i in range(3)]
        hi_ready, lo_ready, weights_used = sem("hi_ready"), sem("lo_ready"), sem("weights_used")

        def at(n, turn, more):
            return n + more if turn is None else turn * 3 + (n + more)

        def split_hi(act, n, width, turn=None):
            s = n % 3
            act.wait_ge(loaded[s], 16 * (n // 3 + 1) if turn is None else turn * 16 + 16 * (n // 3 + 1))
            if n >= 3:
                act.wait_ge(weights_used, at(n, turn, -2))
            act.activation(w_hi[s][:, 0:width], raw[s][:, 0:width], ACT.Copy).then_inc(hi_ready, 1)

        def split_lo(dve, n, width, turn=None):
            s = n % 3
            dve.wait_ge(hi_ready, at(n, turn, 1))
            dve.tensor_tensor(w_lo[s][:, 0:width], raw[s][:, 0:width], w_hi[s][:, 0:width].bitcast(F32),
                              ALU.subtract).then_inc(lo_ready, 1)

        def take(pe, n, turn=None):
            pe.wait_ge(lo_ready, at(n, turn, 1))

        def product(pe, dst, a_hi, a_lo, b_hi, b_lo, start, stop):
            pe.matmul(dst, a_lo, b_hi, start=start, stop=False)
            pe.matmul(dst, a_hi, b_lo, start=False, stop=False)
            return pe.matmul(dst, a_hi, b_hi, start=False, stop=stop)

        def project(pe, n, dst, chunks, width, first=0, total=KC, base=0, ts=range(T), done=True):
            s = n % 3
            for c in range(chunks):
                for t in ts:
                    tok = slice(t * P, (t + 1) * P)
                    k = first + c
                    last = product(pe, dst[t], act_hi[:, base + k, tok], act_lo[:, base + k, tok],
                                   w_hi[s][:, c * width:(c + 1) * width], w_lo[s][:, c * width:(c + 1) * width],
                                   k == 0, k == total - 1)
            if done:
                last.then_inc(weights_used, 1)
            return last

        def project_wide(pe, n, stat_hi, stat_lo, first, start, stop, last_of=None):
            s = n % 3
            for t in range(T):
                for c in range(2):
                    for half in range(2):
                        lo = c * D + half * 512
                        last = product(pe, bank[4 + 2 * t + half][:], stat_hi[:, first + c, t * P:(t + 1) * P],
                                       stat_lo[:, first + c, t * P:(t + 1) * P], w_hi[s][:, lo:lo + 512],
                                       w_lo[s][:, lo:lo + 512], start and c == 0, stop and c == 1)
                if last_of is not None and t == 0:
                    last.then_inc(sem(f"acc_done{last_of}"), 1)
            last.then_inc(weights_used, 1)

        def wait_used(eng, n, turn=None):
            eng.wait_ge(weights_used, at(n, turn, 1))

        def col(k):
            return stats[:, k:k + 1]

        def square(act, s, t):
            if s == 0:
                act.wait_ge(sem(f"x_loaded{t}"), 16)
            else:
                act.wait_ge(sem(f"h_ready{s - 1}"), t + 1)
            act.activation(u[:, t, :], h[:, t, :], ACT.Square,
                           accum_out=col(16 * s + 4 * t)).then_inc(sem(f"pre_squares{s}"), 1)

        def square_acc(act, s, t, n):
            if t == 0:
                act.wait_ge(sem(f"acc_done{s}"), 1)
            else:
                wait_used(act, n)
            for half in range(2):
                act.activation(u[:, t, half * 512:(half + 1) * 512], bank[4 + 2 * t + half][:], ACT.Square,
                               accum_out=col(16 * s + 8 + 4 * t + half)).then_inc(sem(f"post_squares{s}"), 1)

        newton = sb("newton", [P, 4])

        def rstd(tally, dst, total, width):
            dve = tally.eng
            a, y, b = newton[:, 0:1], newton[:, 1:2], newton[:, 2:3]
            tally.link(dve.tensor_scalar(a, total, 1.0 / width, EPS, ALU.mult, ALU.add))
            tally.link(dve.tensor_scalar(b.bitcast(I32), a.bitcast(I32), 1, None, ALU.logical_shift_right))
            tally.link(dve.tensor_scalar(y.bitcast(I32), b.bitcast(I32), -1.0, float(0x5f3759df), ALU.mult, ALU.add))
            for k in range(3):
                tally.link(dve.scalar_tensor_tensor(b, y, a, y, ALU.mult, ALU.mult))
                tally.link(dve.tensor_scalar(b, b, -0.5, 1.5, ALU.mult, ALU.add))
                tally.link(dve.tensor_tensor(dst if k == 2 else y, y, b, ALU.mult))

        def pre_norm(tally, s, t):
            dve = tally.eng
            dve.wait_ge(sem(f"pre_squares{s}"), t + 1)
            rstd(tally, col(16 * s + 4 * t + 1), col(16 * s + 4 * t), D)
            dve.wait_ge(sem(f"gain{2 * s % 4}_loaded"), 16 * (s // 2 + 1))
            dve.scalar_tensor_tensor(u[:, t, :], h[:, t, :], col(16 * s + 4 * t + 1), gain[:, 2 * s % 4, :],
                                     ALU.mult, ALU.mult).then_inc(sem(f"u_ready{s}"), 1)

        def post_norm(tally, s, t):
            dve = tally.eng
            dve.wait_ge(sem(f"post_squares{s}"), 2 * t + 2)
            base = 16 * s + 8 + 4 * t
            tally.link(dve.tensor_tensor(col(base + 2), col(base), col(base + 1), ALU.add))
            rstd(tally, col(base + 3), col(base + 2), D)
            g = (2 * s + 1) % 4
            dve.wait_ge(sem(f"gain{g}_loaded"), 16 * (s // 2 + 1))
            for half in range(2):
                cols = slice(half * 512, (half + 1) * 512)
                ins = dve.scalar_tensor_tensor(u[:, t, cols], bank[4 + 2 * t + half][:], col(base + 3),
                                               gain[:, g, cols], ALU.mult, ALU.mult)
                tally.link(ins)
            dve.tensor_tensor(h[:, t, :], h[:, t, :], u[:, t, :], ALU.add).then_inc(sem(f"h_ready{s}"), 1)

        def turn_pe(pe, name, src, t):
            for b in range(2):
                for c in range(4):
                    k = 4 * b + c
                    last = pe.transpose(bank[2 * t + b][:, c * P:(c + 1) * P], src(t, k), ident[:])
                last.then_inc(sem(f"{name}_turned"), 1)

        def act_part(a, t, b):
            return a[:, 4 * b:4 * b + 4, t * P:(t + 1) * P]

        def turn_act(act, name, t):
            for b in range(2):
                act.wait_ge(sem(f"{name}_turned"), 2 * t + b + 1)
                act.activation(act_part(act_hi, t, b), bank[2 * t + b][:].rearrange("p (c n) -> p c n", c=4),
                               ACT.Copy).then_inc(sem(f"{name}_hi"), 1)

        def turn_dve(dve, name, t):
            for b in range(2):
                dve.wait_ge(sem(f"{name}_hi"), 2 * t + b + 1)
                dve.tensor_tensor(act_part(act_lo, t, b), bank[2 * t + b][:].rearrange("p (c n) -> p c n", c=4),
                                  act_part(act_hi, t, b).bitcast(F32), ALU.subtract).then_inc(sem(f"{name}_lo"), 1)

        def u_chunk(t, k):
            return u[:, t, k * P:(k + 1) * P]

        def lat_chunk(t, k):
            return lat[:, t, k * P:(k + 1) * P]

        def rope(tally, view, half, c, s, shape, last_sem=None):
            dve = tally.eng
            n = 1
            for m in shape:
                n *= m

            def tmp(k):
                rows_ = view.shape[0]
                a = rope_tmp[0:rows_, k, 0:n]
                if len(shape) == 3:
                    return a.rearrange("p (a b c) -> p a b c", a=shape[0], b=shape[1])
                if len(shape) == 2:
                    return a.rearrange("p (a b) -> p a b", a=shape[0])
                return a

            x1, x2 = view[..., 0:half], view[..., half:2 * half]
            tally.link(dve.tensor_tensor(tmp(0), x1, c, ALU.mult))
            tally.link(dve.tensor_tensor(tmp(1), x2, s, ALU.mult))
            tally.link(dve.tensor_tensor(tmp(2), x2, c, ALU.mult))
            tally.link(dve.tensor_tensor(tmp(3), x1, s, ALU.mult))
            tally.link(dve.tensor_tensor(x1, tmp(0), tmp(1), ALU.subtract))
            ins = dve.tensor_tensor(x2, tmp(2), tmp(3), ALU.add)
            if last_sem is None:
                tally.link(ins)
            else:
                ins.then_inc(last_sem, 1)

        def heads_table(tab, heads, step):
            a = tab[:, 0:T, 0:16:step]
            return a.unsqueeze(2).to_broadcast([P, T, heads, 16 // step])

        block = ctx.enter_context(nc.Block())

        @block.sync
        def _(sp):
            def load(n, src, turn=None):
                s = n % 3
                if n >= 3:
                    sp.wait_ge(lo_ready, at(n, turn, -2))
                chunks, width = src.shape[1], src.shape[2]
                dst = raw[s][:, 0:chunks * width].rearrange("p (c n) -> p c n", c=chunks)
                sp.dma_start(dst, src).then_inc(loaded[s], 16)

            def load_ffn(base, layer):
                def gate_up(n, j, half, turn=None):
                    load(n, rows(w_gate_up[layer], 4 * half, 4, bass.ds(j * 2 * FB, 2 * FB)), turn)

                def down(n, j, turn=None):
                    load(n, w_down[layer][bass.ds(j * FB, FB), :].rearrange("(c p) n -> p c n", p=P), turn)

                gate_up(base, 0, 0)
                gate_up(base + 1, 0, 1)
                with sp.Fori(0, STEPS - 1) as turn:
                    gate_up(base + 2, turn + 1, 0, turn)
                    gate_up(base + 3, turn + 1, 1, turn)
                    down(base + 4, turn, turn)
                down(base + 3 * STEPS - 1, STEPS - 1)

            def block_cols(lo, n):
                return slice(lo, lo + n)

            sp.dma_start(h[:, 0, :], x[0:P, :]).then_inc(sem("x_loaded0"), 16)
            for b in range(3):
                for half in range(2):
                    load(NSA_KV + 2 * b + half, rows(nsa_w_in, 4 * half, 4, block_cols(D + 512 * b, 512)))
            load(NSA_GATES, rows(nsa_w_in, 0, KC, block_cols(D + 6 * KVW, GATES)))
            for half in range(2):
                load(NSA_W1K + half, rows(w1_k, 8 * half, 8, block_cols(0, 256)))

            def load_q(n, cols, turn=None):
                for k in range(3):
                    load(n + k, rows(nsa_w_in, 3 * k, (3, 3, 2)[k], cols), turn)

            load_q(NSA_Q0, block_cols(0, KVW))
            for half in range(2):
                load(NSA_W1V + half, rows(w1_v, 8 * half, 8, block_cols(0, 256)))
            with sp.Fori(0, TURNS - 1) as turn:
                load_q(NSA_Q1, bass.ds((turn + 1) * KVW, KVW), turn)
            for m in range(4):
                load(NSA_OUT + m, rows(nsa_w_out, 2 * m, 2, block_cols(0, D)))
            load_ffn(FFN0, 0)

            for b in range(2):
                for half in range(2):
                    load(MLA_IN + 2 * b + half, rows(mla_w_in, 4 * half, 4, block_cols(512 * b, 512)))
            load(MLA_IN + 4, rows(mla_w_in, 0, KC, block_cols(D, ROPE)))

            def load_up(n, q_cols, kv_cols, turn=None):
                for k in range(2):
                    load(n + k, rows(w_q_up, 3 * k, 3, q_cols), turn)
                load(n + 2, rows(w_kv_up, 0, KVC, kv_cols), turn)

            load_up(MLA_UP0, block_cols(0, QUAD * DK), block_cols(0, QUAD * 2 * HD))
            with sp.Fori(0, TURNS - 1) as turn:
                load_up(MLA_UP1, bass.ds((turn + 1) * (QUAD * DK), QUAD * DK),
                        bass.ds((turn + 1) * (QUAD * 2 * HD), QUAD * 2 * HD), turn)
            for m in range(4):
                load(MLA_OUT + m, rows(mla_w_out, 2 * m, 2, block_cols(0, D)))
            load_ffn(FFN1, 1)

            for t in range(T):
                sp.wait_ge(sem("h_ready3"), t + 1)
                sp.dma_start(out[t * P:(t + 1) * P, :], h[:, t, :]).then_inc(sem("stored"), 16)
            sp.wait_ge(sem("stored"), 16 * T)

        @block.gpsimd
        def _(pool):
            pool.dma_start(pos_i[:], positions).then_inc(sem("pos_loaded"), 16)
            pool.dma_start(invf[:], inv_freq.to_broadcast([P, 16])).then_inc(sem("pos_loaded"), 16)
            pool.memset(ident[:], 0.0).then_inc(sem("ident0"), 1)
            pool.wait_ge(sem("ident0"), 1)
            pool.affine_select(out=ident[:], in_=ident[:], compare_op=ALU.not_equal, fill=1.0, base=0,
                               pattern=[[-1, P]], channel_multiplier=1).then_inc(sem("ident"), 1)

            def load_gain(i, layer):
                pool.dma_start(gain[:, i, :], gains[4 * layer + i:4 * layer + i + 1, :].to_broadcast([P, D])) \
                    .then_inc(sem(f"gain{i}_loaded"), 16)

            load_gain(0, 0)
            for v, pe_ in enumerate((pe_k, pe_v)):
                pool.dma_start(peT[:, v, :], pe_).then_inc(sem("pe_loaded"), 16)
            for v, w in enumerate((w2_k, w2_v)):
                pool.dma_start(w2[:, v, :, :], w.rearrange("(c p) n -> p c n", p=P)).then_inc(sem("w2_loaded"), 16)
            pool.memset(mask[:], 0.0).then_inc(sem("masks0"), 1)
            pool.memset(cmask[:], 0.0).then_inc(sem("masks0"), 1)
            pool.memset(anyvalid[:], 1.0).then_inc(sem("masks0"), 1)
            pool.memset(blockmask[:], 1.0).then_inc(sem("masks0"), 1)
            pool.wait_ge(sem("masks0"), 4)
            pool.affine_select(out=mask[:, P:SEQ], in_=mask[:, P:SEQ], compare_op=ALU.is_ge, fill=NEG, base=0,
                               pattern=[[-1, P]], channel_multiplier=1).then_inc(sem("masks"), 1)
            for t in range(T):
                base = t * P - (CMP_LEN - 1)
                pool.affine_select(out=cmask[:, t, :], in_=cmask[:, t, :], compare_op=ALU.is_ge, fill=NEG, base=base,
                                   pattern=[[-CMP_STRIDE, NCMP]], channel_multiplier=1).then_inc(sem("masks"), 1)
                pool.affine_select(out=anyvalid[:, t:t + 1], in_=anyvalid[:, t:t + 1], compare_op=ALU.is_ge,
                                   fill=0.0, base=base, pattern=[[0, 1]],
                                   channel_multiplier=1).then_inc(sem("masks"), 1)
            pool.affine_select(out=blockmask[:], in_=blockmask[:], compare_op=ALU.is_ge, fill=0.0, base=0,
                               pattern=[[-NCMP, QUAD]], channel_multiplier=1).then_inc(sem("blockmask0"), 1)
            pool.wait_ge(sem("blockmask0"), 1)
            pool.affine_select(out=blockmask[:], in_=blockmask[:], compare_op=ALU.is_ge, fill=0.0, base=NCMP - 1,
                               pattern=[[NCMP, QUAD]], channel_multiplier=-1).then_inc(sem("masks"), 1)
            for a in (qT[:], kT, kcT, cT, vbd):
                pool.memset(a, 0.0).then_inc(sem("padded"), 1)
            pool.memset(zero[:].bitcast(F32), 0.0).then_inc(sem("zero"), 1)
            for i in range(1, 4):
                load_gain(i, 0)
            for i, used in enumerate(("u_ready0", "h_ready0", "u_ready1", "h_ready1")):
                pool.wait_ge(sem(used), T)
                load_gain(i, 1)
                if i == 1:
                    pool.dma_start(lat_g[:], lat_gain.to_broadcast([P, D])).then_inc(sem("lat_gain_loaded"), 16)

        @block.tensor
        def _(pe):
            def project_rows(n, dst, chunks, width, total=KC, base=0, firsts=None):
                for k in range(len(chunks)):
                    take(pe, n + k)
                first = 0
                for t in range(T):
                    first = 0
                    for k, c in enumerate(chunks):
                        last = project(pe, n + k, dst, c, width, first, total, base, [t], done=False)
                        first += c
                last.then_inc(weights_used, len(chunks))
                return last

            def ffn(base, s):
                pe.wait_ge(sem(f"u{s}_lo"), 2 * T)
                take(pe, base)
                project(pe, base, [bank[0][:], bank[1][:]], 4, 512, 0)
                take(pe, base + 1)
                project(pe, base + 1, [bank[0][:], bank[1][:]], 4, 512, 4)
                pe.wait_ge(sem("zero"), 1)
                for k in range(4):
                    pe.matmul(bank[4 + k][:], zero[:, 0:P], zero[:], start=True, stop=False)

                def turn_hidden(waits):
                    pe.wait_ge(sem(f"hidden_ready{s}"), waits)
                    for c in range(2):
                        for t in range(T):
                            last = pe.transpose(bank[2][:, c * SEQ + t * P:c * SEQ + (t + 1) * P],
                                                hid[:, t, c * P:(c + 1) * P], ident[:])
                    last.then_inc(sem(f"hidden_turned{s}"), 1)

                with pe.Fori(0, STEPS - 1) as turn:
                    take(pe, base + 2, turn)
                    pe.wait_ge(sem(f"hidden_ready{s}"), turn * T + T)
                    project(pe, base + 2, [bank[0][:], bank[1][:]], 4, 512, 0)
                    turn_hidden(turn * T + T)
                    take(pe, base + 3, turn)
                    project(pe, base + 3, [bank[0][:], bank[1][:]], 4, 512, 4)
                    take(pe, base + 4, turn)
                    pe.wait_ge(sem(f"hiddenT_ready{s}"), turn + 1)
                    project_wide(pe, base + 4, hidT_hi, hidT_lo, 0, False, False)
                turn_hidden(STEPS * T)
                take(pe, base + 3 * STEPS - 1)
                pe.wait_ge(sem(f"hiddenT_ready{s}"), STEPS)
                project_wide(pe, base + 3 * STEPS - 1, hidT_hi, hidT_lo, 0, False, True, last_of=s)

            def turn_u(s):
                for t in range(T):
                    pe.wait_ge(sem(f"u_ready{s}"), t + 1)
                    turn_pe(pe, f"u{s}", u_chunk, t)

            def attend(m, turn, fill):
                nsa = m == "nsa"
                branches = 2 if nsa else 1
                rows_ = P if nsa else DK

                def scores(n):
                    t, i = divmod(n, QUAD)
                    keys = (t + 1) * P
                    q = qT[0:rows_, i, t * P:(t + 1) * P]
                    dst = bank[n % 2][:, 0:branches * keys]
                    if nsa:
                        k = kT[0:rows_, bass.ds(turn, 1), :].squeeze(1).rearrange("p (b s) -> p b s", b=2)[:, :, 0:keys]
                        dst = dst.rearrange("p (b s) -> p b s", b=2)
                    else:
                        k = mkT[0:rows_, i, 0:keys]
                    pe.matmul(dst, q, k, start=True, stop=True).then_inc(sem(f"{m}_scores"), 1)

                def turn_probs(n):
                    t, i = divmod(n, QUAD)
                    pe.wait_ge(sem(f"{m}_exp"), turn * UNITS + n + 1)
                    for b in range(branches * (t + 1)):
                        last = pe.transpose(bank[2 + n % 2][:, b * P:(b + 1) * P],
                                            s_sb[:, n % 2, b * P:(b + 1) * P], ident[:])
                    last.then_inc(sem(f"{m}_turned"), 1)

                def values(n):
                    t, i = divmod(n, QUAD)
                    pe.wait_ge(sem(f"{m}_probsT"), turn * UNITS + n + 1)
                    if n == QUAD:
                        pe.wait_ge(sem(f"{m}_out"), turn * T + 1)
                    for b in range(branches):
                        for kt in range(t + 1):
                            p = pT[:, n % 2, (b * (t + 1) + kt) * P:(b * (t + 1) + kt + 1) * P]
                            if nsa:
                                v = vsw[:, kt, b, bass.ds(turn * HD, HD)]
                            else:
                                v = mv[:, kt, bass.ds(turn * KVW + i * HD, HD)]
                            last = pe.matmul(bank[4 if t == 0 else 7][:, b * KVW + i * HD:b * KVW + (i + 1) * HD],
                                             p, v, start=kt == 0, stop=kt == t)
                    last.then_inc(sem(f"{m}_values"), 1)

                def cmp_scores(t):
                    pe.wait_ge(sem("nsa_out"), turn * T + t + 1)
                    for i in range(QUAD):
                        last = pe.matmul(bank[5][:, i * NCMP:(i + 1) * NCMP], qT[:, i, t * P:(t + 1) * P],
                                         kcT[:, bass.ds(turn * NCMP, NCMP)], start=True, stop=True)
                    last.then_inc(sem("cmp_scores"), 1)

                def cmp_turn(t):
                    pe.transpose(bank[5][0:CROWS, 64:64 + P], cs[:, t, 0:CROWS], ident[:]).then_inc(sem("cmp_turned"), 1)

                def cmp_values(t):
                    pe.wait_ge(sem("cmp_probsT"), turn * T + t + 1)
                    pe.matmul(bank[5][:, KVW:2 * KVW], cT, vbd[:, bass.ds(turn, 1), :].squeeze(1),
                              start=True, stop=True).then_inc(sem("cmp_values"), 1)

                pe.wait_ge(sem(f"{m}_qT"), (turn + 1) * (2 if nsa else 4))
                scores(0)
                if nsa:
                    cmp_scores(0)
                scores(1)
                for n in range(UNITS):
                    if nsa and n in (2, 7):
                        pe.wait_ge(sem("cmp_exp"), turn * T + n // QUAD + 1)
                    turn_probs(n)
                    if n >= 1:
                        values(n - 1)
                    if n + 2 < UNITS:
                        scores(n + 2)
                    if not nsa and n == 6:
                        pe.wait_ge(sem("mla_out"), turn * T + 2)
                    if nsa and n in (2, 7):
                        cmp_turn(n // QUAD)
                    if nsa and n == 3:
                        cmp_values(0)
                    if nsa and n == 5:
                        cmp_scores(1)
                    fill(n)
                if fill is not no_fill:
                    wait_queries(m, turn + 1)
                values(UNITS - 1)
                if fill is not no_fill:
                    turn_queries(m)
                if nsa:
                    cmp_values(1)

            def no_fill(n):
                pass

            def wait_queries(m, turn):
                pe.wait_ge(sem(f"{m}_roped"), turn + 1)
                if m == "mla":
                    pe.wait_ge(sem("mla_kv_out"), (turn + 1) * 2 * T)

            def turn_queries(m):
                nsa = m == "nsa"
                rows_ = HD if nsa else DK
                for t in range(T):
                    for i in range(QUAD):
                        last = pe.transpose(bank[t][0:rows_, i * P:(i + 1) * P],
                                            qs[:, t, i * rows_:(i + 1) * rows_], ident[:])
                    last.then_inc(sem(f"{m}_q_turned"), 1)
                if not nsa:
                    for t in range(T):
                        for i in range(QUAD):
                            last = pe.transpose(bank[5 + t][0:rows_, i * P:(i + 1) * P], mk[:, t, i, :], ident[:])
                        last.then_inc(sem(f"{m}_q_turned"), 1)

            pe.wait_ge(sem("ident"), 1)
            turn_u(0)
            pe.wait_ge(sem("u0_lo"), 2 * T)

            def kv_block(b):
                for half in range(2):
                    take(pe, NSA_KV + 2 * b + half)
                    project(pe, NSA_KV + 2 * b + half, [bank[2 * b][:], bank[2 * b + 1][:]], 4, 512, 4 * half)

            kv_block(0)
            kv_block(1)
            pe.wait_ge(sem("kvc_out"), T)
            for v in range(2):
                for t in range(T):
                    for g in range(4):
                        src = kvc[:, t, (v * 4 + g) * 2 * HD:(v * 4 + g + 1) * 2 * HD]
                        last = pe.transpose(bank[(6, 7, 0, 1)[2 * v + t]][:, g * P:(g + 1) * P], src, ident[:])
                    last.then_inc(sem("c_turned"), 1)
            kv_block(2)
            pe.wait_ge(sem("ksv_out"), 2 * T)
            project_rows(NSA_GATES, [bank[2][:, t * GATES:(t + 1) * GATES] for t in range(T)], [KC], GATES)
            pe.wait_ge(sem("blk_lo"), 1)
            pe.wait_ge(sem("c2T_v"), 2)

            def compress(v, n, dst):
                for half in range(2):
                    take(pe, n + half)
                    s = (n + half) % 3
                    for c in range(8):
                        k = 8 * half + c
                        last = product(pe, dst, blk_hi[:, k, :], blk_lo[:, k, :], w_hi[s][:, c * 256:(c + 1) * 256],
                                       w_lo[s][:, c * 256:(c + 1) * 256], k == 0, k == CK - 1)
                    last.then_inc(weights_used, 1)

            compress(0, NSA_W1K, bank[1][0:CROWS, 0:256])
            pe.wait_ge(sem("ks_roped"), 1)
            pe.wait_ge(sem("c2T_v"), 1)
            for b in range(2):
                for t in range(T):
                    for g in range(QUAD):
                        lo = b * KVW + g * HD
                        last = pe.transpose(bank[(3, 4, 5, 0)[2 * b + t]][0:HD, g * P:(g + 1) * P],
                                            kstage[:, t, lo:lo + HD], ident[:])
                    last.then_inc(sem("k_turned"), 1)
            pe.wait_ge(sem("c2T_k"), 2)
            project_rows(NSA_Q0, [bank[6][:, t * KVW:(t + 1) * KVW] for t in range(T)], [3, 3, 2], KVW)
            pe.wait_ge(sem("blk_lo"), 2)
            compress(1, NSA_W1V, bank[7][0:CROWS, 0:256])
            pe.wait_ge(sem("gates_exp"), 1)
            for v in range(2):
                pe.wait_ge(sem("gelu_done"), v + 1)
                if v == 1:
                    pe.wait_ge(sem("kT_out"), 1)
                for c in range(2):
                    last = pe.transpose(bank[2 + v][:, c * 64:c * 64 + CROWS], hidc[0:CROWS, v, c * P:(c + 1) * P],
                                        ident[0:CROWS, 0:CROWS])
                last.then_inc(sem("hidc_turned"), 1)
            pe.wait_ge(sem("hidcT_out"), 1)
            pe.wait_ge(sem("w2_loaded"), 32)
            pe.wait_ge(sem("kT_out"), 4)
            for c in range(2):
                last = pe.matmul(bank[4][0:CROWS, 0:HD], hidcT[:, c, :], w2[:, 0, c, :], start=c == 0, stop=c == 1)
            last.then_inc(sem("kcmp_done"), 1)
            pe.wait_ge(sem("hidcT_out"), 3)
            for g in range(TURNS):
                for c in range(2):
                    rep = hidcT_rep[:, c, g, :, :].rearrange("p i n -> p (i n)")
                    last = pe.matmul(bank[7][0:CROWS, g * HD:(g + 1) * HD], rep, w2[:, 1, c, :], start=c == 0,
                                     stop=c == 1)
            last.then_inc(sem("vcmp_done"), 1)
            wait_queries("nsa", 0)
            turn_queries("nsa")
            pe.wait_ge(sem("kcmp_roped"), 1)
            pe.transpose(bank[5][0:HD, 0:CROWS], kcs[0:CROWS, :], ident[0:CROWS, 0:CROWS]).then_inc(sem("kcmp_turned"), 1)
            pe.wait_ge(sem("nsa_out"), 1)
            pe.wait_ge(sem("kcT_out"), 1)
            pe.wait_ge(sem("padded"), 5)

            with pe.Fori(0, TURNS - 1) as turn:
                def fill(n):
                    if n not in (1, 4):
                        return
                    t = n // 4
                    for k in range(3):
                        if t == 0:
                            take(pe, NSA_Q1 + k, turn)
                        last = project(pe, NSA_Q1 + k, [bank[6][:, a * KVW:(a + 1) * KVW] for a in range(T)],
                                       (3, 3, 2)[k], KVW, 3 * k, KC, 0, [t], done=False)
                    if t == 1:
                        last.then_inc(weights_used, 3)

                attend("nsa", turn, fill)
            attend("nsa", TURNS - 1, no_fill)

            def output(n, m, s):
                for t in range(T):
                    pe.wait_ge(sem(f"{m}_out"), T * (TURNS - 1) + t + 2)
                    turn_pe(pe, f"o{s}", u_chunk, t)
                pe.wait_ge(sem(f"o{s}_lo"), 2 * T)
                for k in range(4):
                    take(pe, n + k)
                    project_wide(pe, n + k, act_hi, act_lo, 2 * k, k == 0, k == 3, last_of=s if k == 3 else None)

            output(NSA_OUT, "nsa", 0)
            turn_u(1)
            ffn(FFN0, 1)

            turn_u(2)
            pe.wait_ge(sem("u2_lo"), 2 * T)
            for b in range(2):
                for half in range(2):
                    take(pe, MLA_IN + 2 * b + half)
                    project(pe, MLA_IN + 2 * b + half, [bank[2 * b][:], bank[2 * b + 1][:]], 4, 512, 4 * half)
            project_rows(MLA_IN + 4, [bank[4][:, t * ROPE:(t + 1) * ROPE] for t in range(T)], [KC], ROPE)
            for t in range(T):
                pe.wait_ge(sem("lat_ready"), t + 1)
                turn_pe(pe, "lat", lat_chunk, t)
            pe.wait_ge(sem("lat_lo"), 2 * T)

            def up_q(n, k, turn=None):
                take(pe, n + k, turn)
                project(pe, n + k, [bank[5][:, 0:QUAD * DK], bank[6][:, 0:QUAD * DK]], 3, QUAD * DK, 3 * k, QC)

            def up_kv(n, turn=None):
                take(pe, n + 2, turn)
                pe.wait_ge(sem("mla_q_out"), T if turn is None else turn * T + 2 * T)
                project(pe, n + 2, [bank[5][:], bank[6][:]], KVC, 512, 0, KVC, QC)

            up_q(MLA_UP0, 0)
            up_q(MLA_UP0, 1)
            up_kv(MLA_UP0)
            wait_queries("mla", 0)
            turn_queries("mla")
            with pe.Fori(0, TURNS - 1) as turn:
                def fill(n):
                    if n in (1, 3):
                        up_q(MLA_UP1, n // 2, turn)
                    if n == 4:
                        up_kv(MLA_UP1, turn)

                attend("mla", turn, fill)
            attend("mla", TURNS - 1, no_fill)
            output(MLA_OUT, "mla", 2)
            turn_u(3)
            ffn(FFN1, 3)
        @block.scalar
        def _(act):
            chain = Tally(act, sem("act_chain"))
            act.dma_start(h[:, 1, :], x[P:2 * P, :]).then_inc(sem("x_loaded1"), 16)

            def copy(dst, src):
                return act.activation(dst, src, ACT.Copy)

            def output_norm_ffn(m, s, w_tiles, ffn_tiles):
                for t in range(T):
                    turn_act(act, f"o{s}", t)
                split_hi(act, w_tiles + 3, SLOT)
                split_hi(act, ffn_tiles, SLOT)
                split_hi(act, ffn_tiles + 1, SLOT)
                for t in range(T):
                    square_acc(act, s, t, w_tiles + 3)
                for t in range(T):
                    square(act, s + 1, t)
                for t in range(T):
                    turn_act(act, f"u{s + 1}", t)
                split_hi(act, ffn_tiles + 2, SLOT)

            def ffn(base, s):
                def gated(j, n, turn=None):
                    wait_used(act, n, turn)
                    for t in range(T):
                        act.activation(silu[:, t, :], bank[t][:, 0:FB], ACT.Silu).then_inc(sem(f"silu_ready{s}"), 1)

                def hidden_hi(j):
                    act.wait_ge(sem(f"hidden_turned{s}"), j + 1)
                    copy(hidT_hi[:].rearrange("p c s -> p (c s)"), bank[2][:]).then_inc(sem(f"hiddenT_hi{s}"), 1)

                gated(0, base + 1)
                with act.Fori(0, STEPS - 1) as turn:
                    split_hi(act, base + 3, SLOT, turn)
                    hidden_hi(turn)
                    split_hi(act, base + 4, SLOT, turn)
                    split_hi(act, base + 5, SLOT, turn)
                    gated(turn + 1, base + 3, turn)
                return hidden_hi

            def attend(m, turn, splits, last):
                nsa = m == "nsa"
                branches = 2 if nsa else 1
                scale = SEL_SCALE if nsa else MLA_SCALE

                def exps(n):
                    t, i = divmod(n, QUAD)
                    keys = (t + 1) * P
                    act.wait_ge(sem(f"{m}_masked"), turn * UNITS + n + 1)
                    for b in range(branches):
                        v = s_sb[:, n % 2, b * keys:(b + 1) * keys]
                        ins = act.activation(v, v, ACT.Exp, bias=nmax[:, n % 2, b:b + 1], scale=scale,
                                             accum_out=rsum[:, t, i, b + 1:b + 2])
                    ins.then_inc(sem(f"{m}_exp"), 1)

                def cmp_exp(t):
                    act.wait_ge(sem("cmp_masked"), turn * T + t + 1)
                    act.activation(cs[:, t, 0:CROWS], cs[:, t, 0:CROWS], ACT.Exp, scale=scale) \
                        .then_inc(sem("cmp_exp"), 1)

                def probs(n):
                    t = n // QUAD
                    width = branches * (t + 1) * P
                    act.wait_ge(sem(f"{m}_turned"), turn * UNITS + n + 1)
                    copy(pT[:, n % 2, 0:width], bank[2 + n % 2][:, 0:width]).then_inc(sem(f"{m}_probsT"), 1)

                def cmp_probs(t):
                    act.wait_ge(sem("cmp_turned"), turn * T + t + 1)
                    copy(cT[0:CROWS, :], bank[5][0:CROWS, 64:64 + P]).then_inc(sem("cmp_probsT"), 1)

                exps(0)
                splits(0)
                exps(1)
                if nsa:
                    cmp_exp(0)
                splits(1)
                for n in range(UNITS):
                    probs(n)
                    if n == 0:
                        splits(2)
                    if nsa and n == 7:
                        cmp_probs(1)
                    if n + 2 < UNITS:
                        exps(n + 2)
                    if nsa and n == 2:
                        cmp_probs(0)
                    if nsa and n == 5:
                        cmp_exp(1)
                    if not last:
                        if nsa and n == 4:
                            q_out(m, turn + 1, NSA_Q1 + 2, turn)
                        if not nsa and n == 3:
                            q_out(m, turn + 1, MLA_UP1 + 1, turn)
                        if not nsa and n == 4:
                            kv_out(turn + 1, MLA_UP1 + 2, turn)
                if not last:
                    queries_out(m, turn + 1)

            def q_out(m, to, n, turn=None):
                wait_used(act, n, turn)
                if m == "nsa":
                    for t in range(T):
                        copy(qs[:, t, 0:KVW], bank[6][:, t * KVW:(t + 1) * KVW]).then_inc(sem("nsa_q_out"), 1)
                else:
                    for t in range(T):
                        copy(qs[:, t, :], bank[5 + t][:, 0:QUAD * DK]).then_inc(sem("mla_q_out"), 1)

            def kv_out(to, n, turn=None):
                wait_used(act, n, turn)
                for t in range(T):
                    src = bank[5 + t][:].rearrange("p (i n) -> p i n", i=QUAD)
                    copy(mk[:, t, :, 0:NOPE], src[:, :, 0:NOPE]).then_inc(sem("mla_kv_out"), 1)
                    copy(mv[:, t, bass.ds(to * KVW, KVW)].rearrange("p (i n) -> p i n", i=QUAD), src[:, :, NOPE:]) \
                        .then_inc(sem("mla_kv_out"), 1)

            def queries_out(m, to):
                per = T if m == "nsa" else 2 * T
                r = HD if m == "nsa" else DK
                for k in range(per):
                    t = k % T
                    act.wait_ge(sem(f"{m}_q_turned"), to * per + k + 1)
                    dst, src = (qT, bank[t]) if k < T else (mkT, bank[5 + t])
                    copy(dst[0:r, :, t * P:(t + 1) * P], src[0:r, :].rearrange("p (i s) -> p i s", i=QUAD)) \
                        .then_inc(sem(f"{m}_qT"), 1)

            act.wait_ge(sem("angles"), 2)
            act.activation(sin[:].rearrange("p t k -> p (t k)"), ang[:, 0, :], ACT.Sin).then_inc(sem("tables"), 1)
            act.activation(cos[:].rearrange("p t k -> p (t k)"), ang[:, 1, :], ACT.Sin).then_inc(sem("tables"), 1)

            for t in range(T):
                square(act, 0, t)
            for n in range(3):
                split_hi(act, n, SLOT)
            for t in range(T):
                turn_act(act, "u0", t)
            split_hi(act, 3, SLOT)
            wait_used(act, NSA_KV + 1)
            for t in range(T):
                copy(kvc[:, t, :].rearrange("p (g r n) -> p g r n", g=8, r=2),
                     bank[t][:].rearrange("p (g n) -> p g n", g=8).unsqueeze(2).to_broadcast([P, 8, 2, HD])) \
                    .then_inc(sem("kvc_out"), 1)
            split_hi(act, 4, SLOT)

            def ksv_out(b):
                wait_used(act, NSA_KV + 2 * b + 1)
                for t in range(T):
                    src = bank[2 * b + t]
                    copy(kstage[:, t, (b - 1) * KVW:b * KVW], src[:, 0:KVW]).then_inc(sem("ksv_out"), 1)
                    copy(vsw[:, t, b - 1, :], src[:, KVW:]).then_inc(sem("ksv_out"), 1)

            split_hi(act, 5, SLOT)
            ksv_out(1)
            split_hi(act, 6, KC * GATES)
            for t in range(T):
                act.wait_ge(sem("c_turned"), t + 1)
                src = bank[6 + t][:].rearrange("p (g s) -> p g s", g=4)
                copy(c2T[0][0:HD, :, t * P:(t + 1) * P], src[0:HD]).then_inc(sem("c2T_k_half"), 1)
                skip = 1 if t == 0 else 0
                copy(c2T[0][HD:P, :, t * P + skip - 1:(t + 1) * P - 1], src[HD:P, :, skip:]) \
                    .then_inc(sem("c2T_k"), 1)
            split_hi(act, 7, SLOT)
            act.wait_ge(sem("blk_sum"), 1)
            copy(blk_hi[:].rearrange("p c n -> p (c n)"), blkf).then_inc(sem("blk_hi"), 1)
            ksv_out(2)
            split_hi(act, 8, SLOT)
            wait_used(act, NSA_GATES)
            act.activation(gates.rearrange("p t n -> p (t n)"), bank[2][:, 0:T * GATES], ACT.Exp, scale=-1.0) \
                .then_inc(sem("gates_exp"), 1)
            split_hi(act, 9, 3 * KVW)
            act.wait_ge(sem("padded"), 5)
            for k in range(2):
                act.wait_ge(sem("k_turned"), k + 1)
                copy(kT[0:HD, :, k * P:(k + 1) * P], bank[(3, 4)[k]][0:HD, :].rearrange("p (g s) -> p g s", g=QUAD)) \
                    .then_inc(sem("kT_out"), 1)
            split_hi(act, 10, 3 * KVW)
            split_hi(act, 11, 2 * KVW)
            act.wait_ge(sem("blk_sum"), 2)
            wait_used(act, NSA_W1K + 1)
            copy(blk_hi[:].rearrange("p c n -> p (c n)"), blkf).then_inc(sem("blk_hi"), 1)
            act.activation(hidc[0:CROWS, 0, :], bank[1][0:CROWS, 0:256], ACT.Gelu_apprx_tanh) \
                .then_inc(sem("gelu_done"), 1)
            q_out("nsa", 0, NSA_Q0 + 2)
            split_hi(act, 12, SLOT)
            split_hi(act, 13, SLOT)
            wait_used(act, NSA_W1V + 1)
            act.activation(hidc[0:CROWS, 1, :], bank[7][0:CROWS, 0:256], ACT.Gelu_apprx_tanh) \
                .then_inc(sem("gelu_done"), 1)
            act.wait_ge(sem("hidc_turned"), 1)
            copy(hidcT, bank[2][:, 0:128].rearrange("p (c n) -> p c n", c=2)[:, :, 0:CROWS]) \
                .then_inc(sem("hidcT_out"), 1)
            act.wait_ge(sem("hidc_turned"), 2)
            for c in range(2):
                src = bank[3][:, c * 64:c * 64 + CROWS].rearrange("p (g n) -> p g n", g=TURNS)
                copy(hidcT_rep[:, c], src.unsqueeze(2).to_broadcast([P, TURNS, QUAD, NCMP])) \
                    .then_inc(sem("hidcT_out"), 1)
            queries_out("nsa", 0)
            act.wait_ge(sem("kcmp_turned"), 1)
            copy(kcT[0:HD, :], bank[5][0:HD, 0:CROWS]).then_inc(sem("kcT_out"), 1)

            with act.Fori(0, TURNS - 1) as turn:
                attend("nsa", turn, lambda k: split_hi(act, NSA_Q1 + k, (3, 3, 2)[k] * KVW, turn), False)
            attend("nsa", TURNS - 1, lambda k: split_hi(act, NSA_OUT + k, SLOT), True)
            output_norm_ffn("nsa", 0, NSA_OUT, FFN0)
            hidden_hi = ffn(FFN0, 1)
            split_hi(act, MLA_IN, SLOT)
            split_hi(act, MLA_IN + 1, SLOT)
            hidden_hi(STEPS - 1)

            for t in range(T):
                square_acc(act, 1, t, FFN0 + 3 * STEPS - 1)
            for t in range(T):
                square(act, 2, t)
            for t in range(T):
                turn_act(act, "u2", t)
            split_hi(act, MLA_IN + 2, SLOT)
            split_hi(act, MLA_IN + 3, SLOT)
            wait_used(act, MLA_IN + 1)
            for t in range(T):
                copy(lat[:, t, 0:512], bank[t][:]).then_inc(sem("lat_out"), 1)
            split_hi(act, MLA_IN + 4, KC * ROPE)
            wait_used(act, MLA_IN + 3)
            for t in range(T):
                copy(lat[:, t, 512:1024], bank[2 + t][:]).then_inc(sem("lat_out"), 1)
            split_hi(act, MLA_UP0, 3 * QUAD * DK)
            for t in range(T):
                act.wait_ge(sem("lat_out"), 3 + t)
                act.activation(u[:, t, 0:QLAT], lat[:, t, 0:QLAT], ACT.Square,
                               accum_out=lstats[:, 2 * t:2 * t + 1]).then_inc(sem("lat_squares"), 1)
                act.activation(u[:, t, QLAT:D], lat[:, t, QLAT:D], ACT.Square,
                               accum_out=lstats[:, 2 * t + 1:2 * t + 2]).then_inc(sem("lat_squares"), 1)
            wait_used(act, MLA_IN + 4)
            copy(lat[:, :, D:D + ROPE], bank[4][:, 0:T * ROPE].rearrange("p (t n) -> p t n", t=T)) \
                .then_inc(sem("lat_out"), 1)
            split_hi(act, MLA_UP0 + 1, 3 * QUAD * DK)
            split_hi(act, MLA_UP0 + 2, KVC * 512)
            for t in range(T):
                turn_act(act, "lat", t)
            q_out("mla", 0, MLA_UP0 + 1)
            kv_out(0, MLA_UP0 + 2)
            queries_out("mla", 0)
            widths = (3 * QUAD * DK, 3 * QUAD * DK, KVC * 512)
            with act.Fori(0, TURNS - 1) as turn:
                attend("mla", turn, lambda k: split_hi(act, MLA_UP1 + k, widths[k], turn), False)
            attend("mla", TURNS - 1, lambda k: split_hi(act, MLA_OUT + k, SLOT), True)
            output_norm_ffn("mla", 2, MLA_OUT, FFN1)
            hidden_hi = ffn(FFN1, 3)
            hidden_hi(STEPS - 1)
            for t in range(T):
                square_acc(act, 3, t, TILES - 1)

        @block.vector
        def _(dve):
            chain = Tally(dve, sem("dve_chain"))

            def output_norm_ffn(s, w_tiles, ffn_tiles):
                for t in range(T):
                    turn_dve(dve, f"o{s}", t)
                split_lo(dve, w_tiles + 3, SLOT)
                split_lo(dve, ffn_tiles, SLOT)
                split_lo(dve, ffn_tiles + 1, SLOT)
                for t in range(T):
                    post_norm(chain, s, t)
                for t in range(T):
                    pre_norm(chain, s + 1, t)
                for t in range(T):
                    turn_dve(dve, f"u{s + 1}", t)
                split_lo(dve, ffn_tiles + 2, SLOT)

            def ffn(base, s):
                def hidden(j):
                    for t in range(T):
                        dve.wait_ge(sem(f"silu_ready{s}"), j * T + t + 1)
                        dve.tensor_tensor(hid[:, t, :], silu[:, t, :], bank[t][:, FB:2 * FB], ALU.mult) \
                            .then_inc(sem(f"hidden_ready{s}"), 1)

                def hidden_lo(j):
                    dve.wait_ge(sem(f"hiddenT_hi{s}"), j + 1)
                    dve.tensor_tensor(hidT_lo[:].rearrange("p c s -> p (c s)"), bank[2][:],
                                      hidT_hi[:].rearrange("p c s -> p (c s)").bitcast(F32), ALU.subtract) \
                        .then_inc(sem(f"hiddenT_ready{s}"), 1)

                hidden(0)
                with dve.Fori(0, STEPS - 1) as turn:
                    split_lo(dve, base + 3, SLOT, turn)
                    hidden_lo(turn)
                    split_lo(dve, base + 4, SLOT, turn)
                    split_lo(dve, base + 5, SLOT, turn)
                    hidden(turn + 1)
                return hidden_lo

            def attend(m, turn, splits, last):
                nsa = m == "nsa"
                branches = 2 if nsa else 1
                scale = SEL_SCALE if nsa else MLA_SCALE

                def masked(n):
                    t, i = divmod(n, QUAD)
                    keys = (t + 1) * P
                    dve.wait_ge(sem(f"{m}_scores"), turn * UNITS + n + 1)
                    dve.memset(waited[:], 0.0)
                    for b in range(branches):
                        ins = dve.tensor_tensor_reduce(s_sb[:, n % 2, b * keys:(b + 1) * keys],
                                                       bank[n % 2][:, b * keys:(b + 1) * keys],
                                                       mask[:, SEQ - keys:SEQ], 1.0, NEG * 2, ALU.add, ALU.max,
                                                       smax[:, n % 2, b:b + 1])
                    chain.link(ins)
                    dve.tensor_scalar(nmax[:, n % 2, 0:branches], smax[:, n % 2, 0:branches], -scale, None,
                                      ALU.mult).then_inc(sem(f"{m}_masked"), 1)

                def cmp_masked(t):
                    dve.wait_ge(sem("cmp_scores"), turn * T + t + 1)
                    c3 = cs[:, t, 0:CROWS].rearrange("p (i n) -> p i n", i=QUAD)
                    chain.link(dve.tensor_tensor(c3, bank[5][:, 0:CROWS].rearrange("p (i n) -> p i n", i=QUAD),
                                                 cmask[:, t, :].unsqueeze(1).to_broadcast([P, QUAD, NCMP]), ALU.add))
                    chain.link(dve.tensor_reduce(cmax, c3, AX.X, ALU.max))
                    dve.tensor_tensor(c3, c3, cmax.unsqueeze(2).to_broadcast([P, QUAD, NCMP]), ALU.subtract) \
                        .then_inc(sem("cmp_masked"), 1)

                def out(t):
                    dve.wait_ge(sem(f"{m}_values"), turn * UNITS + QUAD * (t + 1))
                    o = bank[4 if t == 0 else 7]
                    dst = u[:, t, bass.ds(turn * KVW, KVW)].rearrange("p (i n) -> p i n", i=QUAD)

                    def by_head(a):
                        return a.rearrange("p (i n) -> p i n", i=QUAD)

                    def factor(b):
                        return fac[:, t, :, b:b + 1].to_broadcast([P, QUAD, HD])

                    if not nsa:
                        chain.link(dve.reciprocal(fac[:, t, :, 1], rsum[:, t, :, 1]))
                        dve.tensor_tensor(dst, by_head(o[:, 0:KVW]), factor(1), ALU.mult).then_inc(sem("mla_out"), 1)
                        return
                    chain.link(dve.tensor_reduce(rsum[:, t, :, 0],
                                                 cs[:, t, 0:CROWS].rearrange("p (i n) -> p i n", i=QUAD), AX.X,
                                                 ALU.add))
                    f = fac[:, t, :, :].rearrange("p i b -> p (i b)")
                    chain.link(dve.reciprocal(f, rsum[:, t, :, :].rearrange("p i b -> p (i b)")))
                    chain.link(dve.tensor_tensor(f, f, gates[:, t, bass.ds(turn * 3 * QUAD, 3 * QUAD)], ALU.mult))
                    chain.link(dve.tensor_scalar(fac[:, t, :, 0], fac[:, t, :, 0], anyvalid[:, t:t + 1], None,
                                                 ALU.mult))
                    dve.tensor_tensor(by_head(o_tmp[:, 0, :]), by_head(o[:, 0:KVW]), factor(1), ALU.mult)
                    chain.link(dve.tensor_tensor(by_head(o_tmp[:, 1, :]), by_head(o[:, KVW:]), factor(2), ALU.mult))
                    dve.wait_ge(sem("cmp_values"), turn * T + t + 1)
                    dve.tensor_tensor(by_head(o_tmp[:, 2, :]), by_head(bank[5][:, KVW:]), factor(0), ALU.mult)
                    chain.link(dve.tensor_tensor(o_tmp[:, 0, :], o_tmp[:, 0, :], o_tmp[:, 1, :], ALU.add))
                    dve.tensor_tensor(dst, by_head(o_tmp[:, 0, :]), by_head(o_tmp[:, 2, :]), ALU.add) \
                        .then_inc(sem("nsa_out"), 1)

                masked(0)
                splits(0)
                masked(1)
                if nsa:
                    cmp_masked(0)
                splits(1)
                masked(2)
                splits(2)
                for n in range(3, 6):
                    masked(n)
                if nsa:
                    out(0)
                    masked(6)
                    masked(7)
                    cmp_masked(1)
                    if not last:
                        rotate(m, turn + 1)
                else:
                    if not last:
                        rotate(m, turn + 1)
                    out(0)
                    masked(6)
                    masked(7)
                out(1)

            def rotate(m, to):
                dve.wait_ge(sem(f"{m}_q_out"), to * T + T)
                if m == "nsa":
                    chain_view = qs[:, :, 0:KVW].rearrange("p t (i n) -> p t i n", i=QUAD)
                    rope(chain, chain_view, 8, heads_table(cos, QUAD, 2), heads_table(sin, QUAD, 2), [T, QUAD, 8],
                         sem("nsa_roped"))
                else:
                    view = qs[:].rearrange("p t (i n) -> p t i n", i=QUAD)[:, :, :, NOPE:]
                    rope(chain, view, 16, heads_table(cos, QUAD, 1), heads_table(sin, QUAD, 1), [T, QUAD, 16],
                         sem("mla_roped"))

            dve.wait_ge(sem("pos_loaded"), 32)
            chain.link(dve.tensor_copy(pos_f[:], pos_i[:]))
            a0 = ang[:, 0, :].rearrange("p (t k) -> p t k", t=T + 1)
            chain.link(dve.tensor_tensor(a0, pos_f[:].unsqueeze(2).to_broadcast([P, T + 1, 16]),
                                         invf[:].unsqueeze(1).to_broadcast([P, T + 1, 16]), ALU.mult))
            a0, a1, a2 = (ang[:, k, :] for k in range(3))
            chain.link(dve.tensor_scalar(a1, a0, 1.0 / TWO_PI, ROUND, ALU.mult, ALU.add))
            chain.link(dve.tensor_scalar(a2, a1, -ROUND, None, ALU.add))
            for part in two_pi_parts():
                chain.link(dve.scalar_tensor_tensor(a0, a2, -part, a0, ALU.mult, ALU.add))
            limit = 3.1415925
            chain.link(dve.tensor_scalar(a0, a0, limit, -limit, ALU.min, ALU.max))
            chain.link(dve.tensor_scalar(a1, a0, -1.0, None, ALU.mult))
            dve.tensor_tensor(a2, a0, a1, ALU.max).then_inc(sem("angles"), 1)
            dve.wait_ge(sem("angles"), 1)
            dve.tensor_scalar(a1, a2, -1.0, math.pi / 2, ALU.mult, ALU.add).then_inc(sem("angles"), 1)

            for t in range(T):
                pre_norm(chain, 0, t)
            for n in range(3):
                split_lo(dve, n, SLOT)
            for t in range(T):
                turn_dve(dve, "u0", t)
            split_lo(dve, 3, SLOT)
            split_lo(dve, 4, SLOT)
            split_lo(dve, 5, SLOT)
            split_lo(dve, 6, KC * GATES)

            def block_sum(v):
                src = c2T[v]
                starts = src[:, :, 0:CMP_STRIDE * NCMP].rearrange("p g (n l) -> p l g n", l=CMP_STRIDE)
                for half in range(2):
                    part = src[:, :, CMP_STRIDE * half:CMP_STRIDE * (half + NCMP)] \
                        .rearrange("p g (n l) -> p l g n", l=CMP_STRIDE)[:, 0:CMP_STRIDE:2]
                    dst = blkf[:, half * 8 * CROWS:(half + 1) * 8 * CROWS].rearrange("p (c g n) -> p c g n", c=8, g=4)
                    pe_ = peT[:, v, 8 * half:8 * half + 8].unsqueeze(2).unsqueeze(3).to_broadcast([P, 8, 4, NCMP])
                    ins = dve.tensor_tensor(dst, part, pe_, ALU.add)
                ins.then_inc(sem("blk_sum"), 1)

            def block_lo(v):
                dve.wait_ge(sem("blk_hi"), v + 1)
                dve.tensor_tensor(blk_lo[:].rearrange("p c n -> p (c n)"), blkf,
                                  blk_hi[:].rearrange("p c n -> p (c n)").bitcast(F32), ALU.subtract) \
                    .then_inc(sem("blk_lo"), 1)

            dve.wait_ge(sem("pe_loaded"), 32)
            dve.wait_ge(sem("c2T_k"), T)
            dve.wait_ge(sem("c2T_k_half"), T)
            block_sum(0)
            split_lo(dve, 7, SLOT)
            for t in range(T):
                dve.wait_ge(sem("c_turned"), T + t + 1)
                src = bank[t][:].rearrange("p (g s) -> p g s", g=4)
                dve.tensor_copy(c2T[1][0:HD, :, t * P:(t + 1) * P], src[0:HD])
                skip = 1 if t == 0 else 0
                dve.tensor_copy(c2T[1][HD:P, :, t * P + skip - 1:(t + 1) * P - 1], src[HD:P, :, skip:]) \
                    .then_inc(sem("c2T_v"), 1)
            block_lo(0)
            dve.wait_ge(sem("ksv_out"), 4 * T)
            dve.wait_ge(sem("tables"), 2)
            view = kstage.rearrange("p t (i n) -> p t i n", n=HD)
            rope(chain, view, 8, heads_table(cos, 2 * QUAD, 2), heads_table(sin, 2 * QUAD, 2), [T, 2 * QUAD, 8],
                 sem("ks_roped"))
            split_lo(dve, 8, SLOT)
            dve.wait_ge(sem("gates_exp"), 1)
            gf = gates.rearrange("p t n -> p (t n)")
            chain.link(dve.tensor_scalar(gf, gf, 1.0, None, ALU.add))
            chain.link(dve.reciprocal(gf, gf))
            split_lo(dve, 9, 3 * KVW)
            dve.wait_ge(sem("c2T_v"), T)
            block_sum(1)
            dve.wait_ge(sem("padded"), 5)
            for k in range(2, 4):
                dve.wait_ge(sem("k_turned"), k + 1)
                dve.tensor_copy(kT[0:HD, :, k * P:(k + 1) * P],
                                bank[(5, 0)[k - 2]][0:HD, :].rearrange("p (g s) -> p g s", g=QUAD)) \
                    .then_inc(sem("kT_out"), 1)
            split_lo(dve, 10, 3 * KVW)
            split_lo(dve, 11, 2 * KVW)
            block_lo(1)
            rotate("nsa", 0)
            split_lo(dve, 12, SLOT)
            split_lo(dve, 13, SLOT)
            dve.wait_ge(sem("kcmp_done"), 1)
            chain.link(dve.tensor_copy(kcs[0:CROWS, :], bank[4][0:CROWS, 0:HD]))
            rope(chain, kcs[0:CROWS, :], 8, cos[0:CROWS, T, 0:16:2], sin[0:CROWS, T, 0:16:2], [8], sem("kcmp_roped"))
            dve.wait_ge(sem("vcmp_done"), 1)
            dve.wait_ge(sem("masks"), 2 * T + 2)
            for g in range(TURNS):
                ins = dve.tensor_tensor(
                    vbd[0:CROWS, g, :].rearrange("p (i n) -> p i n", i=QUAD),
                    bank[7][0:CROWS, g * HD:(g + 1) * HD].unsqueeze(1).to_broadcast([CROWS, QUAD, HD]),
                    blockmask[0:CROWS, :].unsqueeze(2).to_broadcast([CROWS, QUAD, HD]), ALU.mult)
            ins.then_inc(sem("nsa_out"), 1)

            dve.wait_ge(sem("masks"), 2 * T + 2)
            with dve.Fori(0, TURNS - 1) as turn:
                chain.enter(turn, NSA_LINKS)
                attend("nsa", turn, lambda k: split_lo(dve, NSA_Q1 + k, (3, 3, 2)[k] * KVW, turn), False)
            chain.leave(TURNS - 1)
            attend("nsa", TURNS - 1, lambda k: split_lo(dve, NSA_OUT + k, SLOT), True)
            output_norm_ffn(0, NSA_OUT, FFN0)
            hidden_lo = ffn(FFN0, 1)
            split_lo(dve, MLA_IN, SLOT)
            split_lo(dve, MLA_IN + 1, SLOT)
            hidden_lo(STEPS - 1)

            for t in range(T):
                post_norm(chain, 1, t)
            for t in range(T):
                pre_norm(chain, 2, t)
            for t in range(T):
                turn_dve(dve, "u2", t)
            split_lo(dve, MLA_IN + 2, SLOT)
            split_lo(dve, MLA_IN + 3, SLOT)
            split_lo(dve, MLA_IN + 4, KC * ROPE)
            split_lo(dve, MLA_UP0, 3 * QUAD * DK)
            dve.wait_ge(sem("lat_gain_loaded"), 16)
            for t in range(T):
                dve.wait_ge(sem("lat_squares"), 2 * t + 2)
                for part, (lo, hi) in enumerate(((0, QLAT), (QLAT, D))):
                    rstd(chain, lstats[:, 4 + 2 * t + part:5 + 2 * t + part], lstats[:, 2 * t + part:2 * t + part + 1],
                         hi - lo)
                    ins = dve.scalar_tensor_tensor(lat[:, t, lo:hi], lat[:, t, lo:hi],
                                                   lstats[:, 4 + 2 * t + part:5 + 2 * t + part], lat_g[:, lo:hi],
                                                   ALU.mult, ALU.mult)
                ins.then_inc(sem("lat_ready"), 1)
            dve.wait_ge(sem("lat_out"), 5)
            rope(chain, lat[:, :, D:D + ROPE], 16, cos[:, 0:T, :], sin[:, 0:T, :], [T, 16])
            for t in range(T):
                ins = dve.tensor_copy(mk[:, t, :, NOPE:],
                                      lat[:, t, D:D + ROPE].unsqueeze(1).to_broadcast([P, QUAD, ROPE]))
            ins.then_inc(sem("mla_out"), 1)
            split_lo(dve, MLA_UP0 + 1, 3 * QUAD * DK)
            split_lo(dve, MLA_UP0 + 2, KVC * 512)
            for t in range(T):
                turn_dve(dve, "lat", t)
            rotate("mla", 0)
            widths = (3 * QUAD * DK, 3 * QUAD * DK, KVC * 512)
            with dve.Fori(0, TURNS - 1) as turn:
                chain.enter(turn, MLA_LINKS)
                attend("mla", turn, lambda k: split_lo(dve, MLA_UP1 + k, widths[k], turn), False)
            chain.leave(TURNS - 1)
            attend("mla", TURNS - 1, lambda k: split_lo(dve, MLA_OUT + k, SLOT), True)
            output_norm_ffn(2, MLA_OUT, FFN1)
            hidden_lo = ffn(FFN1, 3)
            hidden_lo(STEPS - 1)
            for t in range(T):
                post_norm(chain, 3, t)


def kernel(x, positions, ln_mix_pre, ln_mix_post, ln_ffn_pre, ln_ffn_post, ffn_w_gate, ffn_w_up, ffn_w_down,
           nsa_w_in, nsa_cmp_pe_k, nsa_cmp_w1_k, nsa_cmp_w2_k, nsa_cmp_pe_v, nsa_cmp_w1_v, nsa_cmp_w2_v, nsa_w_out,
           mla_w_in, mla_q_norm, mla_kv_norm, mla_w_q_up, mla_w_kv_up, mla_w_out, **unused):
    import numpy as np
    import concourse.bacc as bacc
    from concourse.bass_utils import run_bass_kernel_spmd as run

    def stacked(parts, axis):
        return np.stack([np.asarray(p) for p in parts], axis=axis)

    layers = 2
    pos = np.asarray(positions)[0]
    gate_up = stacked([np.asarray(w).reshape(layers, D, STEPS, FB) for w in (ffn_w_gate, ffn_w_up)], 3)
    arrays = {
        "x": np.asarray(x)[0],
        "positions": stacked([pos[0:P], pos[P:SEQ],
                              np.resize(np.concatenate([pos[CMP_LEN - 1::CMP_STRIDE]] * 4), P)], 1),
        "inv_freq": (np.float32(500000.0) ** (-np.arange(16, dtype=np.float32) / np.float32(16)))
        .astype(np.float32).reshape(1, 16),
        "gains": stacked([ln_mix_pre, ln_mix_post, ln_ffn_pre, ln_ffn_post], 1).reshape(4 * layers, D),
        "lat_gain": np.concatenate([np.asarray(mla_q_norm), np.asarray(mla_kv_norm)], axis=1),
        "nsa_w_in": np.asarray(nsa_w_in)[0],
        "pe_k": np.ascontiguousarray(np.asarray(nsa_cmp_pe_k)[0].reshape(CK, P).T),
        "pe_v": np.ascontiguousarray(np.asarray(nsa_cmp_pe_v)[0].reshape(CK, P).T),
        "w1_k": np.asarray(nsa_cmp_w1_k)[0], "w1_v": np.asarray(nsa_cmp_w1_v)[0],
        "w2_k": np.asarray(nsa_cmp_w2_k)[0], "w2_v": np.asarray(nsa_cmp_w2_v)[0],
        "nsa_w_out": np.asarray(nsa_w_out)[0],
        "mla_w_in": np.asarray(mla_w_in)[0], "w_q_up": np.asarray(mla_w_q_up)[0],
        "w_kv_up": np.asarray(mla_w_kv_up)[0], "mla_w_out": np.asarray(mla_w_out)[0],
        "w_gate_up": gate_up.reshape(layers, D, 2 * F),
        "w_down": np.asarray(ffn_w_down),
    }
    arrays = {name: np.ascontiguousarray(a) for name, a in arrays.items()}
    nc = bacc.Bacc("TRN2", target_bir_lowering=False, num_devices=1)
    args = {name: nc.dram_tensor(f"in_{name}", a.shape, mybir.dt.from_np(a.dtype), kind="ExternalInput").ap()
            for name, a in arrays.items()}
    out = nc.dram_tensor("out", (SEQ, D), F32, kind="ExternalOutput").ap()
    trunk(nc, out=out, **args)
    result = run(nc, [{f"in_{name}": a for name, a in arrays.items()}], core_ids=[0])
    return result.results[0]["out"].reshape(1, SEQ, D)
```

```python
import math
from contextlib import ExitStack

import concourse.bass as bass
from concourse import mybir
from concourse.alu_op_type import AluOpType as ALU

F32 = mybir.dt.float32
F32R = mybir.dt.float32r
I32 = mybir.dt.int32
ACT = mybir.ActivationFunctionType
AX = mybir.AxisListType

P = 128
SEQ, D, F = 256, 1024, 2816
T = SEQ // P
KC = D // P
EPS = 1e-6
NEG = -1e30
HD = 64
HEADS = 16
QUAD = 4
TURNS = HEADS // QUAD
UNITS = T * QUAD
KVW = 256
CMP_STRIDE, CMP_LEN = 16, 32
NCMP = SEQ // CMP_STRIDE - 1
CROWS = QUAD * NCMP
CK = CMP_LEN * HD // P
GATES = 3 * HEADS
NOPE, ROPE = 64, 32
DK = NOPE + ROPE
QLAT, KVLAT = 768, 256
QC, KVC = QLAT // P, KVLAT // P
FB = 256
STEPS = F // FB
SLOT = 2048
NSA_LINKS, MLA_LINKS = 29, 15

SEL_SCALE = HD ** -0.5
MLA_SCALE = DK ** -0.5
TWO_PI = 2 * math.pi
ROUND = 1.5 * 2.0 ** 23


def two_pi_parts():
    parts, rest = [], TWO_PI
    for _ in range(3):
        unit = 2.0 ** (math.floor(math.log2(rest)) - 7)
        part = math.floor(rest / unit) * unit
        parts.append(part)
        rest -= part
    return parts + [rest]


NSA_KV = 0
NSA_GATES = NSA_KV + 6
NSA_W1K = NSA_GATES + 1
NSA_W1V = NSA_W1K + 2
NSA_Q0 = NSA_W1V + 2
NSA_Q1 = NSA_Q0 + 3
NSA_OUT = NSA_Q1 + 3 * (TURNS - 1)
FFN0 = NSA_OUT + 4
MLA_IN = FFN0 + 3 * STEPS
MLA_UP0 = MLA_IN + 5
MLA_UP1 = MLA_UP0 + 3
MLA_OUT = MLA_UP1 + 3 * (TURNS - 1)
FFN1 = MLA_OUT + 4
TILES = FFN1 + 3 * STEPS


class Tally:

    def __init__(self, eng, sem):
        self.eng, self.sem, self.n, self.turn, self.per = eng, sem, 0, None, 0

    def link(self, ins):
        ins.then_inc(self.sem, 1)
        self.n += 1
        self.eng.wait_ge(self.sem, self.n if self.turn is None else self.turn * self.per + self.n)

    def enter(self, turn, per):
        self.turn, self.per, self.at = turn, per, self.n

    def leave(self, turns):
        assert self.n - self.at == self.per, (self.n - self.at, self.per)
        self.turn, self.n = None, self.at + self.per * turns


def trunk(nc, x, positions, inv_freq, gains, lat_gain, nsa_w_in, pe_k, pe_v, w1_k, w1_v, w2_k, w2_v, nsa_w_out,
          mla_w_in, w_q_up, w_kv_up, mla_w_out, w_gate_up, w_down, out):
    with ExitStack() as ctx:
        def sb(name, shape, dt=F32):
            return ctx.enter_context(nc.sbuf_tensor(name, shape, dt))

        sems = {}

        def sem(name):
            if name not in sems:
                sems[name] = ctx.enter_context(nc.semaphore(name))
            return sems[name]

        raw = [sb(f"raw{i}", [P, SLOT]) for i in range(3)]
        w_hi = [sb(f"w_hi{i}", [P, SLOT], F32R) for i in range(3)]
        w_lo = [sb(f"w_lo{i}", [P, SLOT], F32R) for i in range(3)]
        act_hi = sb("act_hi", [P, KC, SEQ], F32R)
        act_lo = sb("act_lo", [P, KC, SEQ], F32R)
        h = sb("h", [P, T, D])
        u = sb("u", [P, T, D])
        gain = sb("gain", [P, 4, D])
        stats = sb("stats", [P, 64])
        ident = sb("ident", [P, P])
        mask = sb("mask", [P, SEQ])
        zero = sb("zero", [P, 512], F32R)
        cos = sb("cos", [P, T + 1, 16])
        sin = sb("sin", [P, T + 1, 16])
        rope_tmp = sb("rope_tmp", [P, 4, 128])
        eps = sb("eps", [P, 1])
        warm = sb("warm", [P, 1])
        hidT_hi = sb("hidT_hi", [P, 2, SEQ], F32R)
        hidT_lo = sb("hidT_lo", [P, 2, SEQ], F32R)
        qs = sb("qs", [P, T, QUAD * DK])
        qT = sb("qT", [P, QUAD, SEQ])
        s_sb = sb("s_sb", [P, 2, 512])
        pT = sb("pT", [P, 2, 512])
        silu = pT[:, 0, :].rearrange("p (t n) -> p t n", t=T)
        hid = pT[:, 1, :].rearrange("p (t n) -> p t n", t=T)
        smax = sb("smax", [P, 3, 2])
        nmax = sb("nmax", [P, 3, 2])
        waited = sb("waited", [P, 1])
        rsum = sb("rsum", [P, T, QUAD, 3])
        fac = sb("fac", [P, T, QUAD, 3])
        lat_g = sb("lat_g", [P, D])
        o_tmp = lat_g[:, 0:3 * KVW].rearrange("p (b n) -> p b n", b=3)
        big = sb("big", [P, 10240])

        def carve(sizes):
            at, parts = 0, []
            for n in sizes:
                parts.append(big[:, at:at + n])
                at += n
            assert at <= 10240, at
            return parts

        ks_, kT_, vs_, kc2_, vc2_, blkf_, w2_, vbd_, cs_, hidc_, hidcT_, small_ = carve(
            [T * 512, QUAD * 512, T * 512, 4 * SEQ, 4 * SEQ, CK * CROWS, 2 * 2 * HD, TURNS * KVW, T * 64,
             2 * 256, 2 * CROWS + 2 * TURNS * CROWS, 448])
        kvc = u[:]
        kstage = ks_.rearrange("p (t n) -> p t n", t=T)
        kT = kT_.rearrange("p (g n) -> p g n", g=QUAD)
        vsw = vs_.rearrange("p (t b n) -> p t b n", t=T, b=2)
        c2T = [a.rearrange("p (g s) -> p g s", g=4) for a in (kc2_, vc2_)]
        blkf = blkf_
        w2 = w2_.rearrange("p (v c n) -> p v c n", v=2, c=2)
        vbd = vbd_.rearrange("p (g n) -> p g n", g=TURNS)
        cs = cs_.rearrange("p (t n) -> p t n", t=T)
        hidc = hidc_.rearrange("p (v n) -> p v n", v=2)
        hidcT = hidcT_[:, 0:2 * CROWS].rearrange("p (c n) -> p c n", c=2)
        hidcT_rep = hidcT_[:, 2 * CROWS:].rearrange("p (c g i n) -> p c g i n", c=2, g=TURNS, i=QUAD)
        kcs, kcT, cT = small_[:, 0:64], small_[:, 64:124], small_[:, 128:256]
        gates = small_[:, 256:256 + T * GATES].rearrange("p (t n) -> p t n", t=T)
        peT = small_[:, 352:384].rearrange("p (v c) -> p v c", v=2)
        cmax = small_[:, 384:388]
        part_hi = sb("part_hi", [P, KC * SEQ], F32R)
        part_lo = sb("part_lo", [P, KC * SEQ], F32R)
        blk_hi, blk_lo = (a[:, 0:CK * CROWS].rearrange("p (c n) -> p c n", c=CK) for a in (part_hi, part_lo))
        cmask = sb("cmask", [P, T, NCMP])
        anyvalid = sb("anyvalid", [P, T])
        blockmask = sb("blockmask", [P, QUAD])
        lat_, mk_, mkT_, mv_, third_ = carve([T * (D + ROPE), T * QUAD * DK, QUAD * SEQ, T * HEADS * HD, 512])
        places = {"nsa": (s_sb[:, 0, :], s_sb[:, 1, :], ks_[:, 0:512]), "mla": (s_sb[:, 0, :], s_sb[:, 1, :], third_)}
        lat_hi, lat_lo = (a[:].rearrange("p (c s) -> p c s", c=KC) for a in (part_hi, part_lo))
        lat = lat_.rearrange("p (t n) -> p t n", t=T)
        mk = mk_.rearrange("p (t i n) -> p t i n", t=T, i=QUAD)
        mkT = mkT_.rearrange("p (i s) -> p i s", i=QUAD)
        mv = mv_.rearrange("p (t n) -> p t n", t=T)
        pos_i = sb("pos_i", [P, T + 1], I32)
        pos_f = sb("pos_f", [P, T + 1])
        invf = sb("invf", [P, 16])
        ang = sb("ang", [P, 3, (T + 1) * 16])
        lstats = sb("lstats", [P, 12])

        bank = [ctx.enter_context(nc.psum_tensor(f"bank{i}", [P, 512], F32)) for i in range(8)]

        def rows(w, c0, n, cols):
            return w[c0 * P:(c0 + n) * P, cols].rearrange("(c p) n -> p c n", p=P)

        loaded = [sem(f"slot{i}_loaded") for i in range(3)]
        hi_ready, lo_ready, weights_used = sem("hi_ready"), sem("lo_ready"), sem("weights_used")

        def at(n, turn, more):
            return n + more if turn is None else turn * 3 + (n + more)

        def split_hi(act, n, width, turn=None):
            s = n % 3
            act.wait_ge(loaded[s], 16 * (n // 3 + 1) if turn is None else turn * 16 + 16 * (n // 3 + 1))
            if n >= 3:
                act.wait_ge(weights_used, at(n, turn, -2))
            act.activation(w_hi[s][:, 0:width], raw[s][:, 0:width], ACT.Copy).then_inc(hi_ready, 1)

        def split_hi_on_pool(pool, n, width):
            s = n % 3
            pool.wait_ge(loaded[s], 16 * (n // 3 + 1))
            pool.wait_ge(weights_used, n - 2)
            pool.tensor_copy(w_hi[s][:, 0:width], raw[s][:, 0:width]).then_inc(hi_ready, 1)

        def split_lo(dve, n, width, turn=None):
            s = n % 3
            dve.wait_ge(hi_ready, at(n, turn, 1))
            dve.tensor_tensor(w_lo[s][:, 0:width], raw[s][:, 0:width], w_hi[s][:, 0:width].bitcast(F32),
                              ALU.subtract).then_inc(lo_ready, 1)

        def split_lo_on_pool(pool, n):
            pool.wait_ge(lo_ready, n)
            split_lo(pool, n, SLOT)

        def wait_pool_split(dve, n):
            dve.wait_ge(lo_ready, n + 1)

        def take(pe, n, turn=None):
            pe.wait_ge(lo_ready, at(n, turn, 1))

        def product(pe, dst, a_hi, a_lo, b_hi, b_lo, start, stop):
            pe.matmul(dst, a_lo, b_hi, start=start, stop=False)
            pe.matmul(dst, a_hi, b_lo, start=False, stop=False)
            return pe.matmul(dst, a_hi, b_hi, start=False, stop=stop)

        def project(pe, n, dst, chunks, width, first=0, total=KC, base=0, ts=range(T), done=True):
            s = n % 3
            for c in range(chunks):
                for t in ts:
                    tok = slice(t * P, (t + 1) * P)
                    k = first + c
                    last = product(pe, dst[t], act_hi[:, base + k, tok], act_lo[:, base + k, tok],
                                   w_hi[s][:, c * width:(c + 1) * width], w_lo[s][:, c * width:(c + 1) * width],
                                   k == 0, k == total - 1)
            if done:
                last.then_inc(weights_used, 1)
            return last

        def project_wide(pe, n, stat_hi, stat_lo, first, start, stop, last_of=None):
            s = n % 3
            for t in range(T):
                for c in range(2):
                    for half in range(2):
                        lo = c * D + half * 512
                        last = product(pe, bank[4 + 2 * t + half][:], stat_hi[:, first + c, t * P:(t + 1) * P],
                                       stat_lo[:, first + c, t * P:(t + 1) * P], w_hi[s][:, lo:lo + 512],
                                       w_lo[s][:, lo:lo + 512], start and c == 0, stop and c == 1)
                if last_of is not None and t == 0:
                    last.then_inc(sem(f"acc_done{last_of}"), 1)
            last.then_inc(weights_used, 1)

        def wait_used(eng, n, turn=None):
            eng.wait_ge(weights_used, at(n, turn, 1))

        def acc(s, t, half):
            k = 2 * t + half
            return bank[(6, 2, 4, 7)[k] if s % 2 == 0 else 4 + k]

        def stat(s, t, k):
            k += 16 * s + 8 * t
            return stats[:, k:k + 1]

        squares = s_sb[:, 0, :]

        def root(tally, s, t, k, name):
            act = tally.eng
            tally.link(act.activation(stat(s, t, k + 2), stat(s, t, k), ACT.Copy, scale=1.0 / D, bias=EPS))
            act.activation(stat(s, t, k + 3), stat(s, t, k + 1), ACT.Sqrt, scale=1.0 / D,
                           bias=stat(s, t, k + 2)).then_inc(sem(f"{name}{s}"), 1)

        def pre_root(tally, s, t):
            act = tally.eng
            for half in range(2):
                if s == 0:
                    act.wait_ge(sem(f"x_loaded{t}"), 16)
                else:
                    act.wait_ge(sem(f"h_ready{s - 1}"), 2 * t + half + 1)
                tally.link(act.activation(squares, h[:, t, half * 512:(half + 1) * 512], ACT.Square,
                                          accum_out=stat(s, t, half)))
            root(tally, s, t, 0, "pre_root")

        def post_root(tally, s, t, n):
            act = tally.eng
            if t == 0:
                act.wait_ge(sem(f"acc_done{s}"), 1)
            else:
                wait_used(act, n)
            for half in range(2):
                if t == 0:
                    if half == 1:
                        act.wait_ge(sem(f"gained{s}"), 1)
                else:
                    act.wait_ge(sem(f"gained{s}"), 3 + half)
                ins = act.activation(squares, acc(s, t, half)[:], ACT.Square, accum_out=stat(s, t, 4 + half))
                if t == 0 and half == 0:
                    ins.then_inc(sem(f"half_squared{s}"), 1)
                    act.wait_ge(sem(f"half_squared{s}"), 1)
                else:
                    tally.link(ins)
            root(tally, s, t, 4, "post_root")

        def wait_gain(dve, k):
            if k == 0:
                dve.wait_ge(sem("first_gain_loaded"), 16)
            else:
                dve.wait_ge(sem(f"gain{k % 4}_loaded"), 16 * (k // 4 + (k % 4 != 0)))

        def gained(dve, s, t, n):
            if t == 0:
                dve.wait_ge(sem(f"acc_done{s}"), 1)
            else:
                wait_used(dve, n)
            g = (2 * s + 1) % 4
            wait_gain(dve, 2 * s + 1)
            for half in ((1, 0) if t == 0 else (0, 1)):
                if t == 0 and half == 0:
                    dve.wait_ge(sem(f"half_squared{s}"), 1)
                cols = slice(half * 512, (half + 1) * 512)
                dve.tensor_tensor(u[:, t, cols], acc(s, t, half)[:], gain[:, g, cols],
                                  ALU.mult).then_inc(sem(f"gained{s}"), 1)

        newton = sb("newton", [P, 2])
        inverted, inverses = [0], {}

        def invert(tally, root_, total, width, rest=EPS, done=None):
            dve = tally.eng
            mean, b = newton[:, 0:1], newton[:, 1:2]
            dve.reciprocal(root_, root_).then_inc(sem("inverted"), 1)
            inverted[0] += 1
            tally.link(dve.tensor_scalar(mean, total, 1.0 / width, rest, ALU.mult, ALU.add))
            dve.wait_ge(sem("inverted"), inverted[0])
            tally.link(dve.scalar_tensor_tensor(b, root_, mean, root_, ALU.mult, ALU.mult))
            tally.link(dve.tensor_scalar(b, b, -0.5, 1.5, ALU.mult, ALU.add))
            ins = dve.tensor_tensor(root_, root_, b, ALU.mult)
            if done is None:
                tally.link(ins)
            else:
                ins.then_inc(done, 1)
                inverses[id(done)] = inverses.get(id(done), 0) + 1
                dve.wait_ge(done, inverses[id(done)])

        def post_invert(tally, s, t):
            tally.eng.wait_ge(sem(f"post_root{s}"), t + 1)
            invert(tally, stat(s, t, 7), stat(s, t, 5), D, stat(s, t, 6))

        def post_norm(tally, s, t, go_on=True):
            dve = tally.eng
            dve.wait_ge(sem(f"gained{s}"), 2 * t + 2)
            for half in range(2):
                cols = slice(half * 512, (half + 1) * 512)
                dve.scalar_tensor_tensor(h[:, t, cols], u[:, t, cols], stat(s, t, 7), h[:, t, cols],
                                         ALU.mult, ALU.add).then_inc(sem(f"h_ready{s}"), 1)
                if go_on:
                    dve.wait_ge(sem(f"h_ready{s}"), 2 * t + half + 1)
                    pre_norm(dve, s + 1, t, half)

        def pre_norm(dve, s, t, half):
            wait_gain(dve, 2 * s)
            cols = slice(half * 512, (half + 1) * 512)
            dve.tensor_tensor(u[:, t, cols], h[:, t, cols], gain[:, 2 * s % 4, cols],
                              ALU.mult).then_inc(sem(f"u_ready{s}"), 1)

        def pre_scale(s, t):
            return stat(s, t, 3)

        def pre_invert(tally, s):
            for t in range(T):
                tally.eng.wait_ge(sem(f"pre_root{s}"), t + 1)
                invert(tally, pre_scale(s, t), stat(s, t, 1), D, stat(s, t, 2), sem(f"pre_inverted{s}"))

        def warm_root(act):
            act.activation(warm[:], eps[:], ACT.Sqrt)

        def warm_exp(act):
            act.activation(warm[:], eps[:], ACT.Exp)

        def warm_silu(act):
            act.activation(warm[:], eps[:], ACT.Silu)

        def boundary_act(tally, s, n, late_tile=None):
            warm_root(tally.eng)
            post_root(tally, s, 0, n)
            if late_tile is not None:
                split_hi(tally.eng, late_tile, SLOT)
            turn_act(tally.eng, f"u{s + 1}", 0)
            post_root(tally, s, 1, n)
            pre_root(tally, s + 1, 0)
            turn_act(tally.eng, f"u{s + 1}", 1, [0])
            pre_root(tally, s + 1, 1)
            turn_act(tally.eng, f"u{s + 1}", 1, [1])

        def boundary_dve(tally, s, n):
            gained(tally.eng, s, 0, n)
            post_invert(tally, s, 0)
            post_norm(tally, s, 0)
            turn_dve(tally.eng, f"u{s + 1}", 0, [0])
            gained(tally.eng, s, 1, n)
            turn_dve(tally.eng, f"u{s + 1}", 0, [1])
            post_invert(tally, s, 1)
            post_norm(tally, s, 1)
            turn_dve(tally.eng, f"u{s + 1}", 1)
            pre_invert(tally, s + 1)

        def turn_pe(pe, name, src, t, halves=range(2), ready=None):
            for b in halves:
                if ready is not None:
                    pe.wait_ge(sem(ready), 2 * t + b + 1)
                for c in range(4):
                    k = 4 * b + c
                    last = pe.transpose(bank[2 * t + b][:, c * P:(c + 1) * P], src(t, k), ident[:])
                last.then_inc(sem(f"{name}_turned"), 1)

        def act_part(a, t, b):
            return a[:, 4 * b:4 * b + 4, t * P:(t + 1) * P]

        def turn_act(act, name, t, halves=range(2)):
            for b in halves:
                act.wait_ge(sem(f"{name}_turned"), 2 * t + b + 1)
                act.activation(act_part(act_hi, t, b), bank[2 * t + b][:].rearrange("p (c n) -> p c n", c=4),
                               ACT.Copy).then_inc(sem(f"{name}_hi"), 1)

        def turn_dve(dve, name, t, halves=range(2)):
            for b in halves:
                dve.wait_ge(sem(f"{name}_hi"), 2 * t + b + 1)
                dve.tensor_tensor(act_part(act_lo, t, b), bank[2 * t + b][:].rearrange("p (c n) -> p c n", c=4),
                                  act_part(act_hi, t, b).bitcast(F32), ALU.subtract).then_inc(sem(f"{name}_lo"), 1)

        def lat_bank(t, b):
            return bank[5 + t if b == 0 else (7, 0)[t]]

        def lat_root(t, part):
            return lstats[:, 6 + 2 * t + part:7 + 2 * t + part]

        PIECES = ((0, 0, 4, 6), (0, 4, 6, 6), (1, 0, 4, 4), (0, 6, 8, 0), (1, 4, 8, 1))

        def piece_views(j, a):
            t, c0, c1, b = PIECES[j]
            return a[:, c0:c1, t * P:(t + 1) * P], bank[b][:, 0:(c1 - c0) * P].rearrange("p (c n) -> p c n", c=c1 - c0)

        def turn_piece(pe, s, j):
            t, c0, c1, b = PIECES[j]
            for c in range(c0, c1):
                last = pe.transpose(bank[b][:, (c - c0) * P:(c - c0 + 1) * P], u_chunk(t, c), ident[:])
            last.then_inc(sem(f"o{s}_turned"), 1)

        def piece_hi(act, s, j):
            dst, src = piece_views(j, act_hi)
            act.wait_ge(sem(f"o{s}_turned"), j + 1)
            act.activation(dst, src, ACT.Copy).then_inc(sem(f"o{s}_hi"), 1)

        def piece_lo(dve, s, j):
            dst, src = piece_views(j, act_lo)
            hi, _ = piece_views(j, act_hi)
            dve.wait_ge(sem(f"o{s}_hi"), j + 1)
            dve.tensor_tensor(dst, src, hi.bitcast(F32), ALU.subtract).then_inc(sem(f"o{s}_lo"), 1)

        def u_chunk(t, k):
            return u[:, t, k * P:(k + 1) * P]

        def rope(tally, view, half, c, s, shape, last_sem=None):
            dve = tally.eng
            n = 1
            for m in shape:
                n *= m

            def tmp(k):
                rows_ = view.shape[0]
                a = rope_tmp[0:rows_, k, 0:n]
                if len(shape) == 3:
                    return a.rearrange("p (a b c) -> p a b c", a=shape[0], b=shape[1])
                if len(shape) == 2:
                    return a.rearrange("p (a b) -> p a b", a=shape[0])
                return a

            x1, x2 = view[..., 0:half], view[..., half:2 * half]
            tally.link(dve.tensor_tensor(tmp(0), x1, c, ALU.mult))
            tally.link(dve.tensor_tensor(tmp(1), x2, s, ALU.mult))
            tally.link(dve.tensor_tensor(tmp(2), x2, c, ALU.mult))
            tally.link(dve.tensor_tensor(tmp(3), x1, s, ALU.mult))
            tally.link(dve.tensor_tensor(x1, tmp(0), tmp(1), ALU.subtract))
            ins = dve.tensor_tensor(x2, tmp(2), tmp(3), ALU.add)
            if last_sem is None:
                tally.link(ins)
            else:
                ins.then_inc(last_sem, 1)

        def heads_table(tab, heads, step):
            a = tab[:, 0:T, 0:16:step]
            return a.unsqueeze(2).to_broadcast([P, T, heads, 16 // step])

        block = ctx.enter_context(nc.Block())

        @block.sync
        def _(sp):
            def load(n, src, turn=None):
                s = n % 3
                if n >= 3:
                    sp.wait_ge(lo_ready, at(n, turn, -2))
                chunks, width = src.shape[1], src.shape[2]
                dst = raw[s][:, 0:chunks * width].rearrange("p (c n) -> p c n", c=chunks)
                sp.dma_start(dst, src).then_inc(loaded[s], 16)

            def load_ffn(base, layer):
                def gate_up(n, j, half, turn=None):
                    load(n, rows(w_gate_up[layer], 4 * half, 4, bass.ds(j * 2 * FB, 2 * FB)), turn)

                def down(n, j, turn=None):
                    load(n, w_down[layer][bass.ds(j * FB, FB), :].rearrange("(c p) n -> p c n", p=P), turn)

                gate_up(base, 0, 0)
                gate_up(base + 1, 0, 1)
                with sp.Fori(0, STEPS - 1) as turn:
                    gate_up(base + 2, turn + 1, 0, turn)
                    gate_up(base + 3, turn + 1, 1, turn)
                    down(base + 4, turn, turn)
                down(base + 3 * STEPS - 1, STEPS - 1)

            def block_cols(lo, n):
                return slice(lo, lo + n)

            sp.dma_start(h[:, 0, :], x[0:P, :]).then_inc(sem("x_loaded0"), 16)
            sp.dma_start(gain[:, 0, :], gains[0:1, :].to_broadcast([P, D])).then_inc(sem("first_gain_loaded"), 16)
            for b in range(3):
                for half in range(2):
                    load(NSA_KV + 2 * b + half, rows(nsa_w_in, 4 * half, 4, block_cols(D + 512 * b, 512)))
                    if b == 0 and half == 0:
                        sp.dma_start(h[:, 1, :], x[P:2 * P, :]).then_inc(sem("x_loaded1"), 16)
            load(NSA_GATES, rows(nsa_w_in, 0, KC, block_cols(D + 6 * KVW, GATES)))
            for first, w in ((NSA_W1K, w1_k), (NSA_W1V, w1_v)):
                for half in range(2):
                    load(first + half, rows(w, 8 * half, 8, block_cols(0, 256)))

            def load_q(n, cols, turn=None):
                for k in range(3):
                    load(n + k, rows(nsa_w_in, 3 * k, (3, 3, 2)[k], cols), turn)

            load_q(NSA_Q0, block_cols(0, KVW))
            with sp.Fori(0, TURNS - 1) as turn:
                load_q(NSA_Q1, bass.ds((turn + 1) * KVW, KVW), turn)
            for m in range(4):
                load(NSA_OUT + m, rows(nsa_w_out, 4 * (m % 2), 4, block_cols(512 * (m // 2), 512)))
            load_ffn(FFN0, 0)

            for b in range(2):
                for half in range(2):
                    load(MLA_IN + 2 * b + half, rows(mla_w_in, 4 * half, 4, block_cols(512 * b, 512)))
            load(MLA_IN + 4, rows(mla_w_in, 0, KC, block_cols(D, ROPE)))

            def load_up(n, q_cols, kv_cols, turn=None):
                for k in range(2):
                    load(n + k, rows(w_q_up, 3 * k, 3, q_cols), turn)
                load(n + 2, rows(w_kv_up, 0, KVC, kv_cols), turn)

            load_up(MLA_UP0, block_cols(0, QUAD * DK), block_cols(0, QUAD * 2 * HD))
            with sp.Fori(0, TURNS - 1) as turn:
                load_up(MLA_UP1, bass.ds((turn + 1) * (QUAD * DK), QUAD * DK),
                        bass.ds((turn + 1) * (QUAD * 2 * HD), QUAD * 2 * HD), turn)
            for m in range(4):
                load(MLA_OUT + m, rows(mla_w_out, 4 * (m % 2), 4, block_cols(512 * (m // 2), 512)))
            load_ffn(FFN1, 1)

            for t in range(T):
                for half in range(2):
                    sp.wait_ge(sem("h_ready3"), 2 * t + half + 1)
                    cols = slice(half * 512, (half + 1) * 512)
                    sp.dma_start(out[t * P:(t + 1) * P, cols], h[:, t, cols]).then_inc(sem("stored"), 16)
            sp.wait_ge(sem("stored"), 16 * 2 * T)

        @block.gpsimd
        def _(pool):
            pool.memset(eps[:], EPS).then_inc(sem("eps"), 1)
            pool.dma_start(pos_i[:], positions).then_inc(sem("pos_loaded"), 16)
            pool.dma_start(invf[:], inv_freq.to_broadcast([P, 16])).then_inc(sem("pos_loaded"), 16)
            pool.memset(ident[:], 0.0).then_inc(sem("ident0"), 1)
            pool.wait_ge(sem("ident0"), 1)
            pool.affine_select(out=ident[:], in_=ident[:], compare_op=ALU.not_equal, fill=1.0, base=0,
                               pattern=[[-1, P]], channel_multiplier=1).then_inc(sem("ident"), 1)

            def load_gain(i, layer):
                pool.dma_start(gain[:, i, :], gains[4 * layer + i:4 * layer + i + 1, :].to_broadcast([P, D])) \
                    .then_inc(sem(f"gain{i}_loaded"), 16)

            for v, pe_ in enumerate((pe_k, pe_v)):
                pool.dma_start(peT[:, v, :], pe_).then_inc(sem("pe_loaded"), 16)
            for v, w in enumerate((w2_k, w2_v)):
                pool.dma_start(w2[:, v, :, :], w.rearrange("(c p) n -> p c n", p=P)).then_inc(sem("w2_loaded"), 16)
            pool.memset(mask[:], 0.0).then_inc(sem("masks0"), 1)
            pool.memset(cmask[:], 0.0).then_inc(sem("masks0"), 1)
            pool.memset(anyvalid[:], 1.0).then_inc(sem("masks0"), 1)
            pool.memset(blockmask[:], 1.0).then_inc(sem("masks0"), 1)
            pool.wait_ge(sem("masks0"), 4)
            pool.affine_select(out=mask[:, P:SEQ], in_=mask[:, P:SEQ], compare_op=ALU.is_ge, fill=NEG, base=0,
                               pattern=[[-1, P]], channel_multiplier=1).then_inc(sem("masks"), 1)
            for t in range(T):
                base = t * P - (CMP_LEN - 1)
                pool.affine_select(out=cmask[:, t, :], in_=cmask[:, t, :], compare_op=ALU.is_ge, fill=NEG, base=base,
                                   pattern=[[-CMP_STRIDE, NCMP]], channel_multiplier=1).then_inc(sem("masks"), 1)
                pool.affine_select(out=anyvalid[:, t:t + 1], in_=anyvalid[:, t:t + 1], compare_op=ALU.is_ge,
                                   fill=0.0, base=base, pattern=[[0, 1]],
                                   channel_multiplier=1).then_inc(sem("masks"), 1)
            pool.affine_select(out=blockmask[:], in_=blockmask[:], compare_op=ALU.is_ge, fill=0.0, base=0,
                               pattern=[[-NCMP, QUAD]], channel_multiplier=1).then_inc(sem("blockmask0"), 1)
            pool.wait_ge(sem("blockmask0"), 1)
            pool.affine_select(out=blockmask[:], in_=blockmask[:], compare_op=ALU.is_ge, fill=0.0, base=NCMP - 1,
                               pattern=[[NCMP, QUAD]], channel_multiplier=-1).then_inc(sem("masks"), 1)
            for a in (qT[:], kT, kcT, cT, vbd):
                pool.memset(a, 0.0).then_inc(sem("padded"), 1)
            pool.memset(zero[:].bitcast(F32), 0.0).then_inc(sem("zero"), 1)
            for i in range(1, 4):
                load_gain(i, 0)

            def attention_splits(first, widths, out_tile):
                pool.wait_ge(hi_ready, first + 3)
                for n in range(first + 3, out_tile):
                    split_hi_on_pool(pool, n, widths[(n - first) % 3])
                for k in range(3):
                    if k == 0 or out_tile == NSA_OUT:
                        split_hi_on_pool(pool, out_tile + k, SLOT)
                    split_lo_on_pool(pool, out_tile + k)

            for i, used in enumerate(("u_ready0", "h_ready0", "u_ready1", "h_ready1")):
                if i == 1:
                    attention_splits(NSA_Q1, tuple(c * KVW for c in (3, 3, 2)), NSA_OUT)
                if i in (1, 3):
                    split_lo_on_pool(pool, (FFN0 + 1, MLA_IN + 1)[i // 2])
                pool.wait_ge(sem(used), 2 * T)
                load_gain(i, 1)
                if i == 1:
                    pool.dma_start(lat_g[:], lat_gain.to_broadcast([P, D])).then_inc(sem("lat_gain_loaded"), 16)
            attention_splits(MLA_UP1, (3 * QUAD * DK, 3 * QUAD * DK, KVC * 512), MLA_OUT)
            split_lo_on_pool(pool, FFN1 + 1)

        @block.tensor
        def _(pe):
            def project_rows(n, dst, chunks, width, total=KC, base=0, firsts=None):
                for t in range(T):
                    first = 0
                    for k, c in enumerate(chunks):
                        if t == 0:
                            take(pe, n + k)
                        last = project(pe, n + k, dst, c, width, first, total, base, [t], done=False)
                        first += c
                last.then_inc(weights_used, len(chunks))
                return last

            def ffn(base, s):
                first_block(s, base)
                pe.wait_ge(sem("zero"), 1)
                for k in range(4):
                    pe.matmul(bank[4 + k][:], zero[:, 0:P], zero[:], start=True, stop=False)

                def turn_hidden(waits):
                    pe.wait_ge(sem(f"hidden_ready{s}"), waits)
                    for c in range(2):
                        for t in range(T):
                            last = pe.transpose(bank[2][:, c * SEQ + t * P:c * SEQ + (t + 1) * P],
                                                hid[:, t, c * P:(c + 1) * P], ident[:])
                    last.then_inc(sem(f"hidden_turned{s}"), 1)

                with pe.Fori(0, STEPS - 1) as turn:
                    take(pe, base + 2, turn)
                    pe.wait_ge(sem(f"hidden_ready{s}"), turn * T + T)
                    project(pe, base + 2, [bank[0][:], bank[1][:]], 4, 512, 0)
                    turn_hidden(turn * T + T)
                    take(pe, base + 3, turn)
                    project(pe, base + 3, [bank[0][:], bank[1][:]], 4, 512, 4)
                    take(pe, base + 4, turn)
                    pe.wait_ge(sem(f"hiddenT_ready{s}"), turn + 1)
                    project_wide(pe, base + 4, hidT_hi, hidT_lo, 0, False, False)
                turn_hidden(STEPS * T)
                take(pe, base + 3 * STEPS - 1)
                pe.wait_ge(sem(f"hiddenT_ready{s}"), STEPS)
                project_wide(pe, base + 3 * STEPS - 1, hidT_hi, hidT_lo, 0, False, True, last_of=s)

            def first_block(s, n):
                def turn_half(t, b):
                    turn_pe(pe, f"u{s}", u_chunk, t, [b], f"u_ready{s}")

                turn_half(0, 0)
                turn_half(0, 1)
                for t in range(T):
                    for k in range(KC):
                        if k % 4 == 0:
                            pe.wait_ge(sem(f"u{s}_lo"), 2 * t + k // 4 + 1)
                            if t == 0:
                                take(pe, n + k // 4)
                        if t == 0 and k == 6:
                            turn_half(1, 0)
                        i, c, tok = (n + k // 4) % 3, k % 4, slice(t * P, (t + 1) * P)
                        last = product(pe, bank[t][:], act_hi[:, k, tok], act_lo[:, k, tok],
                                       w_hi[i][:, c * 512:(c + 1) * 512], w_lo[i][:, c * 512:(c + 1) * 512],
                                       k == 0, k == KC - 1)
                        if t == 1 and c == 3:
                            last.then_inc(weights_used, 1)
                    if t == 0:
                        last.then_inc(sem(f"first_block{s}"), 1)
                        turn_half(1, 1)

            def attend(m, turn, fill, opening=False, early=None):
                nsa = m == "nsa"
                branches = 2 if nsa else 1
                rows_ = P if nsa else DK

                def scores(n, turn=turn):
                    t, i = divmod(n, QUAD)
                    keys = (t + 1) * P
                    q = qT[0:rows_, i, t * P:(t + 1) * P]
                    dst = bank[n % 2][:, 0:branches * keys]
                    if nsa:
                        k = kT[0:rows_, bass.ds(turn, 1), :].squeeze(1).rearrange("p (b s) -> p b s", b=2)[:, :, 0:keys]
                        dst = dst.rearrange("p (b s) -> p b s", b=2)
                    else:
                        k = mkT[0:rows_, i, 0:keys]
                    pe.matmul(dst, q, k, start=True, stop=True).then_inc(sem(f"{m}_scores"), 1)

                def turn_probs(n):
                    t, i = divmod(n, QUAD)
                    pe.wait_ge(sem(f"{m}_exp"), turn * UNITS + n + 1)
                    for b in range(branches * (t + 1)):
                        last = pe.transpose(bank[2 + n % 2][:, b * P:(b + 1) * P],
                                            places[m][n % 3][:, b * P:(b + 1) * P], ident[:])
                    last.then_inc(sem(f"{m}_turned"), 1)

                def values(n):
                    t, i = divmod(n, QUAD)
                    pe.wait_ge(sem(f"{m}_probsT"), turn * UNITS + n + 1)
                    if n == QUAD:
                        pe.wait_ge(sem(f"{m}_out"), turn * T + 1)
                    for b in range(branches):
                        for kt in range(t + 1):
                            p = pT[:, n % 2, (b * (t + 1) + kt) * P:(b * (t + 1) + kt + 1) * P]
                            if nsa:
                                v = vsw[:, kt, b, bass.ds(turn * HD, HD)]
                            else:
                                v = mv[:, kt, bass.ds(turn * KVW + i * HD, HD)]
                            last = pe.matmul(bank[4 if t == 0 else 7][:, b * KVW + i * HD:b * KVW + (i + 1) * HD],
                                             p, v, start=kt == 0, stop=kt == t)
                    last.then_inc(sem(f"{m}_values"), 1)

                def cmp_scores(t):
                    pe.wait_ge(sem("nsa_out"), turn * T + t + 1)
                    for i in range(QUAD):
                        last = pe.matmul(bank[5][:, i * NCMP:(i + 1) * NCMP], qT[:, i, t * P:(t + 1) * P],
                                         kcT[:, bass.ds(turn * NCMP, NCMP)], start=True, stop=True)
                    last.then_inc(sem("cmp_scores"), 1)

                def cmp_turn(t):
                    pe.transpose(bank[5][0:CROWS, 64:64 + P], cs[:, t, 0:CROWS],
                                 ident[:]).then_inc(sem("cmp_turned"), 1)

                def cmp_values(t):
                    pe.wait_ge(sem("cmp_probsT"), turn * T + t + 1)
                    pe.matmul(bank[5][:, KVW:2 * KVW], cT, vbd[:, bass.ds(turn, 1), :].squeeze(1),
                              start=True, stop=True).then_inc(sem("cmp_values"), 1)

                def first_scores(n, turn):
                    if n == 0:
                        pe.wait_ge(sem(f"{m}_qT"), turn * T + T)
                        if not nsa:
                            pe.wait_ge(sem("mla_kT"), turn * T + T)
                    scores(n, turn)

                if opening:
                    first_scores(0, turn)
                    first_scores(1, turn)
                    return
                for n in range(UNITS):
                    if n + 2 < UNITS:
                        pe.wait_ge(sem(f"{m}_masked"), turn * UNITS + n + 1)
                        scores(n + 2)
                    turn_probs(n)
                    if nsa and n in (3, 7):
                        pe.wait_ge(sem("cmp_exp"), turn * T + n // QUAD + 1)
                    if n == 6 and fill is not None:
                        wait_queries(m, turn + 1)
                    if n >= 1:
                        values(n - 1)
                    if not nsa and n == 6:
                        pe.wait_ge(sem("mla_out"), turn * T + 2)
                    if nsa and n in (3, 7):
                        cmp_turn(n // QUAD)
                    if nsa and n == 4:
                        cmp_values(0)
                    if nsa and n in (1, 5):
                        cmp_scores(n // QUAD)
                    if early is not None:
                        early(n)
                    if fill is not None:
                        fill(n)
                        if n == 6:
                            turn_queries(m)
                if fill is not None:
                    first_scores(0, turn + 1)
                values(UNITS - 1)
                if fill is not None:
                    first_scores(1, turn + 1)
                if nsa:
                    cmp_values(1)

            def wait_queries(m, turn):
                pe.wait_ge(sem(f"{m}_roped"), turn + 1)
                if m == "mla":
                    pe.wait_ge(sem("mla_kv_out"), (turn + 1) * 2 * T)

            def turn_queries(m):
                nsa = m == "nsa"
                rows_ = HD if nsa else DK
                for t in range(T):
                    for i in range(QUAD):
                        last = pe.transpose(bank[(0, 6 if nsa else 4)[t]][0:rows_, i * P:(i + 1) * P],
                                            qs[:, t, i * rows_:(i + 1) * rows_], ident[:])
                    last.then_inc(sem(f"{m}_q_turned"), 1)
                if not nsa:
                    for t in range(T):
                        for i in range(QUAD):
                            last = pe.transpose(bank[5 + t][0:rows_, i * P:(i + 1) * P], mk[:, t, i, :], ident[:])
                        last.then_inc(sem("mla_k_turned"), 1)

            pe.wait_ge(sem("ident"), 1)

            def kv_block(b):
                for half in range(2):
                    take(pe, NSA_KV + 2 * b + half)
                    project(pe, NSA_KV + 2 * b + half, [bank[2 * b][:], bank[2 * b + 1][:]], 4, 512, 4 * half)

            first_block(0, NSA_KV)
            kv_block(1)
            pe.wait_ge(sem("kvc_out"), T)
            for v in range(2):
                for t in range(T):
                    for g in range(4):
                        src = kvc[:, t, (v * 4 + g) * 2 * HD:(v * 4 + g + 1) * 2 * HD]
                        last = pe.transpose(bank[(6, 7, 0, 1)[2 * v + t]][:, g * P:(g + 1) * P], src, ident[:])
                    last.then_inc(sem("c_turned"), 1)
            kv_block(2)
            pe.wait_ge(sem("ksv_out"), 2 * T)
            project_rows(NSA_GATES, [bank[2][:, t * GATES:(t + 1) * GATES] for t in range(T)], [KC], GATES)
            pe.wait_ge(sem("blk_lo"), 1)
            pe.wait_ge(sem("c2T_v"), 2)

            def compress(v, n, dst):
                for half in range(2):
                    take(pe, n + half)
                    s = (n + half) % 3
                    for c in range(8):
                        k = 8 * half + c
                        last = product(pe, dst, blk_hi[:, k, :], blk_lo[:, k, :], w_hi[s][:, c * 256:(c + 1) * 256],
                                       w_lo[s][:, c * 256:(c + 1) * 256], k == 0, k == CK - 1)
                    last.then_inc(weights_used, 1)

            compress(0, NSA_W1K, bank[1][0:CROWS, 0:256])
            pe.wait_ge(sem("ks_roped"), 1)
            pe.wait_ge(sem("c2T_v"), 1)
            for b in range(2):
                for t in range(T):
                    for g in range(QUAD):
                        lo = b * KVW + g * HD
                        last = pe.transpose(bank[(3, 4, 5, 0)[2 * b + t]][0:HD, g * P:(g + 1) * P],
                                            kstage[:, t, lo:lo + HD], ident[:])
                    last.then_inc(sem("k_turned"), 1)
            pe.wait_ge(sem("c2T_k"), 2)
            pe.wait_ge(sem("blk_lo"), 2)
            compress(1, NSA_W1V, bank[7][0:CROWS, 0:256])

            def turn_hidc(v):
                pe.wait_ge(sem("gelu_done"), v + 1)
                for c in range(2):
                    last = pe.transpose(bank[2 + v][:, c * 64:c * 64 + CROWS], hidc[0:CROWS, v, c * P:(c + 1) * P],
                                        ident[0:CROWS, 0:CROWS])
                last.then_inc(sem("hidc_turned"), 1)

            pe.wait_ge(sem("gates_exp"), T)
            turn_hidc(0)
            project_rows(NSA_Q0, [bank[6][:, t * KVW:(t + 1) * KVW] for t in range(T)], [3, 3, 2], KVW)
            pe.wait_ge(sem("kT_out"), 1)
            turn_hidc(1)
            pe.wait_ge(sem("hidcT_out"), 1)
            pe.wait_ge(sem("w2_loaded"), 32)
            pe.wait_ge(sem("kT_out"), 4)
            for c in range(2):
                last = pe.matmul(bank[4][0:CROWS, 0:HD], hidcT[:, c, :], w2[:, 0, c, :], start=c == 0, stop=c == 1)
            last.then_inc(sem("kcmp_done"), 1)
            pe.wait_ge(sem("hidcT_out"), 3)
            for g in range(TURNS):
                for c in range(2):
                    rep = hidcT_rep[:, c, g, :, :].rearrange("p i n -> p (i n)")
                    last = pe.matmul(bank[7][0:CROWS, g * HD:(g + 1) * HD], rep, w2[:, 1, c, :], start=c == 0,
                                     stop=c == 1)
            last.then_inc(sem("vcmp_done"), 1)
            wait_queries("nsa", 0)
            turn_queries("nsa")
            pe.wait_ge(sem("kcmp_roped"), 1)
            pe.transpose(bank[5][0:HD, 0:CROWS], kcs[0:CROWS, :],
                         ident[0:CROWS, 0:CROWS]).then_inc(sem("kcmp_turned"), 1)
            pe.wait_ge(sem("nsa_out"), 1)
            pe.wait_ge(sem("kcT_out"), 1)
            pe.wait_ge(sem("padded"), 5)

            def q_fill(first, turn):
                def fill(n):
                    if n >= 4:
                        return
                    t, part = divmod(n, 2)
                    for k in range(4 * part, 4 * part + 4):
                        tile, c = divmod(k, 3)
                        if t == 0 and c == 0:
                            take(pe, first + tile, turn)
                        i, tok, cols = (first + tile) % 3, slice(t * P, (t + 1) * P), slice(c * KVW, (c + 1) * KVW)
                        last = product(pe, bank[6][:, t * KVW:(t + 1) * KVW], act_hi[:, k, tok], act_lo[:, k, tok],
                                       w_hi[i][:, cols], w_lo[i][:, cols], k == 0, k == KC - 1)
                    if n == 3:
                        last.then_inc(weights_used, 3)
                return fill

            def out_product(n, s, t, k, half):
                i, tok = (n + 2 * half + k // 4) % 3, slice(t * P, (t + 1) * P)
                cols = slice(k % 4 * 512, (k % 4 + 1) * 512)
                return product(pe, acc(s, t, half)[:], act_hi[:, k, tok], act_lo[:, k, tok], w_hi[i][:, cols],
                               w_lo[i][:, cols], k == 0, k == KC - 1)

            def early_output(n, m, s):
                begin = 4 if m == "nsa" else 5

                def early(step):
                    if step == 0:
                        pe.wait_ge(sem(f"{m}_out"), T * (TURNS - 2) + 2)
                        turn_piece(pe, s, 0)
                    if step == 2:
                        pe.wait_ge(sem(f"o{s}_lo"), 1)
                        turn_piece(pe, s, 1)
                    if step == begin:
                        pe.wait_ge(sem(f"o{s}_lo"), 2)
                        take(pe, n + 1)
                    if begin <= step < begin + 3:
                        for k in (2 * (step - begin), 2 * (step - begin) + 1):
                            out_product(n, s, 0, k, 0)
                    if step == 7:
                        pe.wait_ge(sem(f"{m}_out"), T * (TURNS - 1) + 2)
                        turn_piece(pe, s, 2)
                        turn_piece(pe, s, 3)
                return early

            def output(n, m, s):
                take(pe, n + 2)
                for k in range(4):
                    out_product(n, s, 0, k, 1)
                pe.wait_ge(sem(f"{m}_out"), T * (TURNS - 1) + 3)
                turn_piece(pe, s, 4)
                pe.wait_ge(sem(f"o{s}_lo"), 4)
                for k in (6, 7):
                    out_product(n, s, 0, k, 0)
                for half in range(2):
                    for t in range(T):
                        if half == 0 and t == 0:
                            continue
                        if half == 0:
                            pe.wait_ge(sem(f"o{s}_lo"), 5)
                        for k in range(4 if half == 1 and t == 0 else 0, KC):
                            if k % 4 == 0 and t == 0:
                                take(pe, n + 2 * half + k // 4)
                            last = out_product(n, s, t, k, half)
                            if t == T - 1 and k % 4 == 3:
                                last.then_inc(weights_used, 1)
                        if half == 1 and t == 0:
                            last.then_inc(sem(f"acc_done{s}"), 1)

            attend("nsa", 0, None, opening=True)
            with pe.Fori(0, TURNS - 2) as turn:
                attend("nsa", turn, q_fill(NSA_Q1, turn))
            attend("nsa", TURNS - 2, q_fill(NSA_Q1 + 3 * (TURNS - 2), None))
            attend("nsa", TURNS - 1, None, early=early_output(NSA_OUT, "nsa", 0))

            output(NSA_OUT, "nsa", 0)
            ffn(FFN0, 1)

            first_block(2, MLA_IN)

            def turn_latents(t, b):
                pe.wait_ge(sem("lat_ready"), 2 * b + t + 1)
                for c in range(4):
                    last = pe.transpose(lat_bank(t, b)[:, c * P:(c + 1) * P],
                                        lat[:, t, (4 * b + c) * P:(4 * b + c + 1) * P], ident[:])
                last.then_inc(sem("lat_turned"), 1)

            def rotary_key(t):
                return project(pe, MLA_IN + 4, [bank[4][:, a * ROPE:(a + 1) * ROPE] for a in range(T)], KC, ROPE,
                               ts=[t], done=t == T - 1)

            take(pe, MLA_IN + 2)
            project(pe, MLA_IN + 2, [bank[2][:], bank[3][:]], 4, 512, 0)
            for t in range(T):
                turn_latents(t, 0)
            take(pe, MLA_IN + 3)
            project(pe, MLA_IN + 3, [bank[2][:], bank[3][:]], 4, 512, 4)
            take(pe, MLA_IN + 4)
            rotary_key(0)
            for t in range(T):
                turn_latents(t, 1)
            rotary_key(1)
            pe.wait_ge(sem("lat_lo"), 2 * T)

            def up_part(n, width, c, first, total, base, done):
                for t in range(T):
                    i, k, tok, cols = n % 3, first + c, slice(t * P, (t + 1) * P), slice(c * width, (c + 1) * width)
                    last = product(pe, bank[5 + t][:, 0:width], lat_hi[:, base + k, tok], lat_lo[:, base + k, tok],
                                   w_hi[i][:, cols], w_lo[i][:, cols], k == 0, k == total - 1)
                if done:
                    last.then_inc(weights_used, 1)

            def up_q(n, k, turn=None):
                take(pe, n + k, turn)
                for c in range(3):
                    up_part(n + k, QUAD * DK, c, 3 * k, QC, 0, c == 2)

            def up_kv(n, to, turn=None):
                take(pe, n + 2, turn)
                pe.wait_ge(sem("mla_q_out"), to * T + T)
                for c in range(KVC):
                    up_part(n + 2, 512, c, 0, KVC, QC, c == KVC - 1)

            up_q(MLA_UP0, 0)
            up_q(MLA_UP0, 1)
            up_kv(MLA_UP0, 0)
            wait_queries("mla", 0)
            turn_queries("mla")
            def up_fill(first, turn, to):
                def fill(n):
                    if n < 3:
                        for k in (2 * n, 2 * n + 1):
                            tile, c = divmod(k, 3)
                            if c == 0:
                                take(pe, first + tile, turn)
                            up_part(first + tile, QUAD * DK, c, 3 * tile, QC, 0, c == 2)
                    elif n == 3:
                        up_kv(first, to, turn)
                return fill

            attend("mla", 0, None, opening=True)
            with pe.Fori(0, TURNS - 2) as turn:
                attend("mla", turn, up_fill(MLA_UP1, turn, turn + 1))
            attend("mla", TURNS - 2, up_fill(MLA_UP1 + 3 * (TURNS - 2), None, TURNS - 1))
            attend("mla", TURNS - 1, None, early=early_output(MLA_OUT, "mla", 2))
            output(MLA_OUT, "mla", 2)
            ffn(FFN1, 3)
        @block.scalar
        def _(act):
            chain = Tally(act, sem("act_chain"))

            def copy(dst, src):
                return act.activation(dst, src, ACT.Copy)

            def scaled(dst, src, scale):
                return act.activation(dst, src, ACT.Copy, scale=scale)

            def output_norm_ffn(m, s, w_tiles, ffn_tiles):
                piece_hi(act, s, 4)
                act.wait_ge(hi_ready, w_tiles + 3)
                split_hi(act, w_tiles + 3, SLOT)
                split_hi(act, ffn_tiles, SLOT)
                boundary_act(chain, s, w_tiles + 3, ffn_tiles + 1)
                split_hi(act, ffn_tiles + 2, SLOT)
                warm_silu(act)

            def ffn(base, s):
                def gated(n, turn=None, first=False):
                    if not first:
                        wait_used(act, n, turn)
                    for t in range(T):
                        if first:
                            if t == 0:
                                act.wait_ge(sem(f"first_block{s}"), 1)
                            else:
                                wait_used(act, n)
                            act.wait_ge(sem(f"pre_inverted{s}"), t + 1)
                        act.activation(silu[:, t, :], bank[t][:, 0:FB], ACT.Silu, scale=pre_scale(s, t)) \
                            .then_inc(sem(f"silu_ready{s}"), 1)

                def hidden_hi(j):
                    act.wait_ge(sem(f"hidden_turned{s}"), j + 1)
                    copy(hidT_hi[:].rearrange("p c s -> p (c s)"), bank[2][:]).then_inc(sem(f"hiddenT_hi{s}"), 1)

                gated(base + 1, first=True)
                with act.Fori(0, STEPS - 1) as turn:
                    split_hi(act, base + 3, SLOT, turn)
                    hidden_hi(turn)
                    split_hi(act, base + 4, SLOT, turn)
                    split_hi(act, base + 5, SLOT, turn)
                    gated(base + 3, turn)
                return hidden_hi

            def attend(m, turn, last, first=None, loop_turn=None):
                nsa = m == "nsa"
                branches = 2 if nsa else 1
                scale = SEL_SCALE if nsa else MLA_SCALE

                def exps(n):
                    t, i = divmod(n, QUAD)
                    keys = (t + 1) * P
                    act.wait_ge(sem(f"{m}_masked"), turn * UNITS + n + 1)
                    for b in range(branches):
                        v = places[m][n % 3][:, b * keys:(b + 1) * keys]
                        ins = act.activation(v, v, ACT.Exp, bias=nmax[:, n % 3, b:b + 1], scale=scale,
                                             accum_out=rsum[:, t, i, b + 1:b + 2])
                    ins.then_inc(sem(f"{m}_exp"), 1)

                def cmp_exp(t):
                    act.wait_ge(sem("cmp_masked"), turn * T + t + 1)
                    act.activation(cs[:, t, 0:CROWS], cs[:, t, 0:CROWS], ACT.Exp, scale=scale) \
                        .then_inc(sem("cmp_exp"), 1)

                def probs(n):
                    t = n // QUAD
                    width = branches * (t + 1) * P
                    act.wait_ge(sem(f"{m}_turned"), turn * UNITS + n + 1)
                    copy(pT[:, n % 2, 0:width], bank[2 + n % 2][:, 0:width]).then_inc(sem(f"{m}_probsT"), 1)

                def cmp_probs(t):
                    act.wait_ge(sem("cmp_turned"), turn * T + t + 1)
                    copy(cT[0:CROWS, :], bank[5][0:CROWS, 64:64 + P]).then_inc(sem("cmp_probsT"), 1)

                exps(0)
                exps(1)
                for n in range(UNITS):
                    probs(n)
                    if nsa and n == 7:
                        cmp_probs(1)
                    if not nsa and not last and n == 4:
                        kv_out(turn + 1, first + 2, loop_turn)
                    if n + 2 < UNITS:
                        exps(n + 2)
                    if last and n in (0, 2):
                        piece_hi(act, 0 if nsa else 2, n // 2)
                    if last and not nsa and n in (0, 3):
                        tile = MLA_OUT + 1 + n // 3
                        act.wait_ge(hi_ready, tile)
                        split_hi(act, tile, SLOT)
                    if last and n == 7:
                        piece_hi(act, 0 if nsa else 2, 2)
                        piece_hi(act, 0 if nsa else 2, 3)
                    if nsa and n == 3:
                        cmp_probs(0)
                    if nsa and n in (1, 5):
                        cmp_exp(n // QUAD)
                    if not last:
                        if n == (3 if nsa else 2):
                            q_out(m, turn + 1, first + (2 if nsa else 1), loop_turn)
                        if n == 6:
                            queries_out(m, turn + 1)

            def q_out(m, to, n, turn=None):
                wait_used(act, n, turn)
                if m == "nsa":
                    for t in range(T):
                        scaled(qs[:, t, 0:KVW], bank[6][:, t * KVW:(t + 1) * KVW], pre_scale(0, t)) \
                            .then_inc(sem("nsa_q_out"), 1)
                else:
                    for t in range(T):
                        act.activation(qs[:, t, :], bank[5 + t][:, 0:QUAD * DK], ACT.Copy,
                                       scale=lat_root(t, 0)).then_inc(sem("mla_q_out"), 1)

            def kv_out(to, n, turn=None):
                wait_used(act, n, turn)
                for t in range(T):
                    src = bank[5 + t][:].rearrange("p (i n) -> p i n", i=QUAD)
                    act.activation(mk[:, t, :, 0:NOPE], src[:, :, 0:NOPE], ACT.Copy,
                                   scale=lat_root(t, 1)).then_inc(sem("mla_kv_out"), 1)
                    act.activation(mv[:, t, bass.ds(to * KVW, KVW)].rearrange("p (i n) -> p i n", i=QUAD),
                                   src[:, :, NOPE:], ACT.Copy, scale=lat_root(t, 1)).then_inc(sem("mla_kv_out"), 1)

            def queries_out(m, to):
                r = HD if m == "nsa" else DK
                for t in range(T):
                    act.wait_ge(sem(f"{m}_q_turned"), to * T + t + 1)
                    src = bank[(0, 6 if m == "nsa" else 4)[t]]
                    copy(qT[0:r, :, t * P:(t + 1) * P], src[0:r, :].rearrange("p (i s) -> p i s", i=QUAD)) \
                        .then_inc(sem(f"{m}_qT"), 1)

            act.wait_ge(sem("eps"), 1)
            warm_root(act)

            pre_root(chain, 0, 0)
            turn_act(act, "u0", 0)
            split_hi(act, 0, SLOT)
            pre_root(chain, 0, 1)
            split_hi(act, 1, SLOT)
            split_hi(act, 2, SLOT)
            turn_act(act, "u0", 1)
            act.wait_ge(sem("angles"), 2)
            act.activation(sin[:].rearrange("p t k -> p (t k)"), ang[:, 0, :], ACT.Sin).then_inc(sem("tables"), 1)
            act.activation(cos[:].rearrange("p t k -> p (t k)"), ang[:, 1, :], ACT.Sin).then_inc(sem("tables"), 1)
            split_hi(act, 3, SLOT)
            wait_used(act, NSA_KV + 1)
            act.wait_ge(sem("pre_inverted0"), T)
            for t in range(T):
                scaled(kvc[:, t, :].rearrange("p (g r n) -> p g r n", g=8, r=2),
                       bank[t][:].rearrange("p (g n) -> p g n", g=8).unsqueeze(2).to_broadcast([P, 8, 2, HD]),
                       pre_scale(0, t)) \
                    .then_inc(sem("kvc_out"), 1)
            split_hi(act, 4, SLOT)

            def ksv_out(b):
                wait_used(act, NSA_KV + 2 * b + 1)
                for t in range(T):
                    src = bank[2 * b + t]
                    scaled(kstage[:, t, (b - 1) * KVW:b * KVW], src[:, 0:KVW], pre_scale(0, t)) \
                        .then_inc(sem("ksv_out"), 1)
                    scaled(vsw[:, t, b - 1, :], src[:, KVW:], pre_scale(0, t)).then_inc(sem("ksv_out"), 1)

            split_hi(act, 5, SLOT)
            ksv_out(1)
            split_hi(act, 6, KC * GATES)
            for t in range(T):
                act.wait_ge(sem("c_turned"), t + 1)
                src = bank[6 + t][:].rearrange("p (g s) -> p g s", g=4)
                copy(c2T[0][0:HD, :, t * P:(t + 1) * P], src[0:HD]).then_inc(sem("c2T_k_half"), 1)
                skip = 1 if t == 0 else 0
                copy(c2T[0][HD:P, :, t * P + skip - 1:(t + 1) * P - 1], src[HD:P, :, skip:]) \
                    .then_inc(sem("c2T_k"), 1)
            split_hi(act, 7, SLOT)
            act.wait_ge(sem("blk_sum"), 1)
            copy(blk_hi[:].rearrange("p c n -> p (c n)"), blkf).then_inc(sem("blk_hi"), 1)
            ksv_out(2)
            split_hi(act, 8, SLOT)
            wait_used(act, NSA_GATES)
            act.wait_ge(sem("gate_scale"), T)
            for t in range(T):
                act.activation(gates[:, t, :], bank[2][:, t * GATES:(t + 1) * GATES], ACT.Exp, scale=stat(0, t, 2)) \
                    .then_inc(sem("gates_exp"), 1)
            split_hi(act, 9, SLOT)
            split_hi(act, 10, SLOT)
            act.wait_ge(sem("blk_sum"), 2)
            wait_used(act, NSA_W1K + 1)
            copy(blk_hi[:].rearrange("p c n -> p (c n)"), blkf).then_inc(sem("blk_hi"), 1)
            act.wait_ge(sem("padded"), 5)
            for k in range(2):
                act.wait_ge(sem("k_turned"), k + 1)
                copy(kT[0:HD, :, k * P:(k + 1) * P], bank[(3, 4)[k]][0:HD, :].rearrange("p (g s) -> p g s", g=QUAD)) \
                    .then_inc(sem("kT_out"), 1)
            act.activation(hidc[0:CROWS, 0, :], bank[1][0:CROWS, 0:256], ACT.Gelu_apprx_tanh) \
                .then_inc(sem("gelu_done"), 1)
            split_hi(act, 11, 3 * KVW)
            split_hi(act, 12, 3 * KVW)
            act.wait_ge(sem("hidc_turned"), 1)
            copy(hidcT, bank[2][:, 0:128].rearrange("p (c n) -> p c n", c=2)[:, :, 0:CROWS]) \
                .then_inc(sem("hidcT_out"), 1)
            wait_used(act, NSA_W1V + 1)
            split_hi(act, 13, 2 * KVW)
            act.activation(hidc[0:CROWS, 1, :], bank[7][0:CROWS, 0:256], ACT.Gelu_apprx_tanh) \
                .then_inc(sem("gelu_done"), 1)
            q_out("nsa", 0, NSA_Q0 + 2)
            act.wait_ge(sem("hidc_turned"), 2)
            for c in range(2):
                src = bank[3][:, c * 64:c * 64 + CROWS].rearrange("p (g n) -> p g n", g=TURNS)
                copy(hidcT_rep[:, c], src.unsqueeze(2).to_broadcast([P, TURNS, QUAD, NCMP])) \
                    .then_inc(sem("hidcT_out"), 1)
            split_hi(act, NSA_Q1, 3 * KVW)
            warm_exp(act)
            queries_out("nsa", 0)
            act.wait_ge(sem("kcmp_turned"), 1)
            copy(kcT[0:HD, :], bank[5][0:HD, 0:CROWS]).then_inc(sem("kcT_out"), 1)
            split_hi(act, NSA_Q1 + 1, 3 * KVW)
            split_hi(act, NSA_Q1 + 2, 2 * KVW)

            with act.Fori(0, TURNS - 2) as turn:
                attend("nsa", turn, False, NSA_Q1, turn)
            attend("nsa", TURNS - 2, False, NSA_Q1 + 3 * (TURNS - 2))
            attend("nsa", TURNS - 1, True)
            output_norm_ffn("nsa", 0, NSA_OUT, FFN0)
            hidden_hi = ffn(FFN0, 1)
            split_hi(act, MLA_IN, SLOT)
            hidden_hi(STEPS - 1)

            split_hi(act, MLA_IN + 1, SLOT)
            boundary_act(chain, 1, FFN0 + 3 * STEPS - 1)
            split_hi(act, MLA_IN + 2, SLOT)
            split_hi(act, MLA_IN + 3, SLOT)
            def lat_squares(k, t, src):
                return act.activation(squares[:, 0:src.shape[1]], src, ACT.Square, scale=pre_scale(2, t),
                                      accum_out=lstats[:, 3 * t + k:3 * t + k + 1])

            def latents_hi(t, b):
                act.wait_ge(sem("lat_turned"), 2 * b + t + 1)
                copy(act_part(lat_hi, t, b), lat_bank(t, b)[:].rearrange("p (c n) -> p c n", c=4)) \
                    .then_inc(sem("lat_hi"), 1)

            act.wait_ge(sem("pre_inverted2"), T)
            wait_used(act, MLA_IN + 1)
            for t in range(T):
                lat_squares(0, t, bank[t][:]).then_inc(sem("lat_squared"), 1)
                act.wait_ge(sem("lat_squared"), t + 1)
            split_hi(act, MLA_IN + 4, KC * ROPE)
            for t in range(T):
                latents_hi(t, 0)
            wait_used(act, MLA_IN + 3)
            for t in range(T):
                chain.link(lat_squares(1, t, bank[2 + t][:, 0:QLAT - 512]))
                lat_squares(2, t, bank[2 + t][:, QLAT - 512:]).then_inc(sem("lat_squared"), 1)
                act.wait_ge(sem("lat_squared"), T + t + 1)
            split_hi(act, MLA_UP0, 3 * QUAD * DK)
            for t in range(T):
                latents_hi(t, 1)
            split_hi(act, MLA_UP0 + 1, 3 * QUAD * DK)
            for t in range(T):
                chain.link(act.activation(lstats[:, 10 + t:11 + t], lstats[:, 3 * t:3 * t + 1], ACT.Copy,
                                          scale=1.0 / QLAT, bias=EPS))
                act.activation(lat_root(t, 0), lstats[:, 3 * t + 1:3 * t + 2], ACT.Sqrt, scale=1.0 / QLAT,
                               bias=lstats[:, 10 + t:11 + t]).then_inc(sem("lat_roots"), 1)
                act.activation(lat_root(t, 1), lstats[:, 3 * t + 2:3 * t + 3], ACT.Sqrt, scale=1.0 / KVLAT,
                               bias=eps[:]).then_inc(sem("lat_roots"), 1)
            wait_used(act, MLA_IN + 4)
            for t in range(T):
                scaled(lat[:, t, D:D + ROPE], bank[4][:, t * ROPE:(t + 1) * ROPE], pre_scale(2, t)) \
                    .then_inc(sem("lat_out"), 1)
            split_hi(act, MLA_UP0 + 2, KVC * 512)
            act.wait_ge(sem("lat_inverted"), 2 * T)
            widths = (3 * QUAD * DK, 3 * QUAD * DK, KVC * 512)
            q_out("mla", 0, MLA_UP0 + 1)
            warm_exp(act)
            kv_out(0, MLA_UP0 + 2)
            split_hi(act, MLA_UP1, widths[0])
            queries_out("mla", 0)
            split_hi(act, MLA_UP1 + 1, widths[1])
            split_hi(act, MLA_UP1 + 2, widths[2])
            with act.Fori(0, TURNS - 2) as turn:
                attend("mla", turn, False, MLA_UP1, turn)
            attend("mla", TURNS - 2, False, MLA_UP1 + 3 * (TURNS - 2))
            attend("mla", TURNS - 1, True)
            output_norm_ffn("mla", 2, MLA_OUT, FFN1)
            hidden_hi = ffn(FFN1, 3)
            hidden_hi(STEPS - 1)
            for t in range(T):
                post_root(chain, 3, t, TILES - 1)

        @block.vector
        def _(dve):
            chain = Tally(dve, sem("dve_chain"))

            def output_norm_ffn(s, w_tiles, ffn_tiles):
                piece_lo(dve, s, 4)
                wait_pool_split(dve, w_tiles + 2)
                split_lo(dve, w_tiles + 3, SLOT)
                split_lo(dve, ffn_tiles, SLOT)
                boundary_dve(chain, s, w_tiles + 3)
                wait_pool_split(dve, ffn_tiles + 1)
                split_lo(dve, ffn_tiles + 2, SLOT)

            def ffn(base, s):
                def hidden(j):
                    for t in range(T):
                        dve.wait_ge(sem(f"silu_ready{s}"), j * T + t + 1)
                        dve.scalar_tensor_tensor(hid[:, t, :], bank[t][:, FB:2 * FB], pre_scale(s, t),
                                                 silu[:, t, :], ALU.mult, ALU.mult) \
                            .then_inc(sem(f"hidden_ready{s}"), 1)

                def hidden_lo(j):
                    dve.wait_ge(sem(f"hiddenT_hi{s}"), j + 1)
                    dve.tensor_tensor(hidT_lo[:].rearrange("p c s -> p (c s)"), bank[2][:],
                                      hidT_hi[:].rearrange("p c s -> p (c s)").bitcast(F32), ALU.subtract) \
                        .then_inc(sem(f"hiddenT_ready{s}"), 1)

                hidden(0)
                with dve.Fori(0, STEPS - 1) as turn:
                    split_lo(dve, base + 3, SLOT, turn)
                    hidden_lo(turn)
                    split_lo(dve, base + 4, SLOT, turn)
                    split_lo(dve, base + 5, SLOT, turn)
                    hidden(turn + 1)
                return hidden_lo

            def attend(m, turn, last, splits=None, opening=False):
                nsa = m == "nsa"
                branches = 2 if nsa else 1
                scale = SEL_SCALE if nsa else MLA_SCALE

                def masked(n, turn=turn):
                    t, i = divmod(n, QUAD)
                    keys = (t + 1) * P
                    dve.wait_ge(sem(f"{m}_scores"), turn * UNITS + n + 1)
                    dve.memset(waited[:], 0.0)
                    for b in range(branches):
                        ins = dve.tensor_tensor_reduce(places[m][n % 3][:, b * keys:(b + 1) * keys],
                                                       bank[n % 2][:, b * keys:(b + 1) * keys],
                                                       mask[:, SEQ - keys:SEQ], 1.0, NEG * 2, ALU.add, ALU.max,
                                                       smax[:, n % 3, b:b + 1])
                    chain.link(ins)
                    dve.tensor_scalar(nmax[:, n % 3, 0:branches], smax[:, n % 3, 0:branches], -scale, None,
                                      ALU.mult).then_inc(sem(f"{m}_masked"), 1)

                def cmp_masked(t):
                    dve.wait_ge(sem("cmp_scores"), turn * T + t + 1)
                    c3 = cs[:, t, 0:CROWS].rearrange("p (i n) -> p i n", i=QUAD)
                    chain.link(dve.tensor_tensor(c3, bank[5][:, 0:CROWS].rearrange("p (i n) -> p i n", i=QUAD),
                                                 cmask[:, t, :].unsqueeze(1).to_broadcast([P, QUAD, NCMP]), ALU.add))
                    chain.link(dve.tensor_reduce(cmax, c3, AX.X, ALU.max))
                    dve.tensor_tensor(c3, c3, cmax.unsqueeze(2).to_broadcast([P, QUAD, NCMP]), ALU.subtract) \
                        .then_inc(sem("cmp_masked"), 1)

                def out(t):
                    o = bank[4 if t == 0 else 7]
                    dst = u[:, t, bass.ds(turn * KVW, KVW)].rearrange("p (i n) -> p i n", i=QUAD)

                    def by_head(a):
                        return a.rearrange("p (i n) -> p i n", i=QUAD)

                    def factor(b):
                        return fac[:, t, :, b:b + 1].to_broadcast([P, QUAD, HD])

                    def values_done():
                        dve.wait_ge(sem(f"{m}_values"), turn * UNITS + QUAD * (t + 1))

                    dve.wait_ge(sem(f"{m}_exp"), turn * UNITS + QUAD * (t + 1))
                    if not nsa:
                        chain.link(dve.reciprocal(fac[:, t, :, 1], rsum[:, t, :, 1]))
                        values_done()
                        dve.tensor_tensor(dst, by_head(o[:, 0:KVW]), factor(1), ALU.mult).then_inc(sem("mla_out"), 1)
                        return
                    dve.wait_ge(sem("cmp_exp"), turn * T + t + 1)
                    chain.link(dve.tensor_reduce(rsum[:, t, :, 0],
                                                 cs[:, t, 0:CROWS].rearrange("p (i n) -> p i n", i=QUAD), AX.X,
                                                 ALU.add))
                    f = fac[:, t, :, :].rearrange("p i b -> p (i b)")
                    chain.link(dve.reciprocal(f, rsum[:, t, :, :].rearrange("p i b -> p (i b)")))
                    chain.link(dve.tensor_tensor(f, f, gates[:, t, bass.ds(turn * 3 * QUAD, 3 * QUAD)], ALU.mult))
                    chain.link(dve.tensor_scalar(fac[:, t, :, 0], fac[:, t, :, 0], anyvalid[:, t:t + 1], None,
                                                 ALU.mult))
                    values_done()
                    dve.tensor_tensor(by_head(o_tmp[:, 0, :]), by_head(o[:, 0:KVW]), factor(1), ALU.mult)
                    chain.link(dve.tensor_tensor(by_head(o_tmp[:, 1, :]), by_head(o[:, KVW:]), factor(2), ALU.mult))
                    dve.wait_ge(sem("cmp_values"), turn * T + t + 1)
                    dve.tensor_tensor(by_head(o_tmp[:, 2, :]), by_head(bank[5][:, KVW:]), factor(0), ALU.mult)
                    chain.link(dve.tensor_tensor(o_tmp[:, 0, :], o_tmp[:, 0, :], o_tmp[:, 1, :], ALU.add))
                    dve.tensor_tensor(dst, by_head(o_tmp[:, 0, :]), by_head(o_tmp[:, 2, :]), ALU.add) \
                        .then_inc(sem("nsa_out"), 1)

                if opening:
                    masked(0)
                    masked(1)
                    return
                for n in range(2, 6):
                    masked(n)
                    if nsa and n == 3:
                        cmp_masked(0)
                    if last and n in (3, 4):
                        piece_lo(dve, 0 if nsa else 2, n - 3)
                if not nsa and not last:
                    rotate(m, turn + 1)
                out(0)
                masked(6)
                if nsa and not last:
                    rotate(m, turn + 1)
                masked(7)
                if nsa:
                    cmp_masked(1)
                if not last:
                    if splits:
                        splits(0)
                    if not nsa:
                        keys_out(turn + 1)
                    if splits:
                        splits(1)
                    masked(0, turn + 1)
                    masked(1, turn + 1)
                    if splits:
                        splits(2)
                if last:
                    piece_lo(dve, 0 if nsa else 2, 2)
                    piece_lo(dve, 0 if nsa else 2, 3)
                out(1)

            def keys_out(to):
                for t in range(T):
                    dve.wait_ge(sem("mla_k_turned"), to * T + t + 1)
                    dve.tensor_copy(mkT[0:DK, :, t * P:(t + 1) * P],
                                    bank[5 + t][0:DK, :].rearrange("p (i s) -> p i s", i=QUAD)) \
                        .then_inc(sem("mla_kT"), 1)

            def rotate(m, to):
                dve.wait_ge(sem(f"{m}_q_out"), to * T + T)
                if m == "nsa":
                    chain_view = qs[:, :, 0:KVW].rearrange("p t (i n) -> p t i n", i=QUAD)
                    rope(chain, chain_view, 8, heads_table(cos, QUAD, 2), heads_table(sin, QUAD, 2), [T, QUAD, 8],
                         sem("nsa_roped"))
                else:
                    view = qs[:].rearrange("p t (i n) -> p t i n", i=QUAD)[:, :, :, NOPE:]
                    rope(chain, view, 16, heads_table(cos, QUAD, 1), heads_table(sin, QUAD, 1), [T, QUAD, 16],
                         sem("mla_roped"))

            dve.wait_ge(sem("x_loaded0"), 16)
            for half in range(2):
                pre_norm(dve, 0, 0, half)
            turn_dve(dve, "u0", 0)
            split_lo(dve, 0, SLOT)
            dve.wait_ge(sem("x_loaded1"), 16)
            for half in range(2):
                pre_norm(dve, 0, 1, half)
            split_lo(dve, 1, SLOT)
            split_lo(dve, 2, SLOT)
            turn_dve(dve, "u0", 1)
            pre_invert(chain, 0)
            for t in range(T):
                ins = dve.tensor_scalar(stat(0, t, 2), pre_scale(0, t), -1.0, None, ALU.mult)
                ins.then_inc(sem("gate_scale"), 1)

            dve.wait_ge(sem("pos_loaded"), 32)
            chain.link(dve.tensor_copy(pos_f[:], pos_i[:]))
            a0 = ang[:, 0, :].rearrange("p (t k) -> p t k", t=T + 1)
            chain.link(dve.tensor_tensor(a0, pos_f[:].unsqueeze(2).to_broadcast([P, T + 1, 16]),
                                         invf[:].unsqueeze(1).to_broadcast([P, T + 1, 16]), ALU.mult))
            a0, a1, a2 = (ang[:, k, :] for k in range(3))
            chain.link(dve.tensor_scalar(a1, a0, 1.0 / TWO_PI, ROUND, ALU.mult, ALU.add))
            chain.link(dve.tensor_scalar(a2, a1, -ROUND, None, ALU.add))
            for part in two_pi_parts():
                chain.link(dve.scalar_tensor_tensor(a0, a2, -part, a0, ALU.mult, ALU.add))
            limit = 3.1415925
            chain.link(dve.tensor_scalar(a0, a0, limit, -limit, ALU.min, ALU.max))
            chain.link(dve.tensor_scalar(a1, a0, -1.0, None, ALU.mult))
            dve.tensor_tensor(a2, a0, a1, ALU.max).then_inc(sem("angles"), 1)
            dve.wait_ge(sem("angles"), 1)
            dve.tensor_scalar(a1, a2, -1.0, math.pi / 2, ALU.mult, ALU.add).then_inc(sem("angles"), 1)

            split_lo(dve, 3, SLOT)
            split_lo(dve, 4, SLOT)
            split_lo(dve, 5, SLOT)
            split_lo(dve, 6, KC * GATES)

            def block_sum(v):
                src = c2T[v]
                starts = src[:, :, 0:CMP_STRIDE * NCMP].rearrange("p g (n l) -> p l g n", l=CMP_STRIDE)
                for half in range(2):
                    part = src[:, :, CMP_STRIDE * half:CMP_STRIDE * (half + NCMP)] \
                        .rearrange("p g (n l) -> p l g n", l=CMP_STRIDE)[:, 0:CMP_STRIDE:2]
                    dst = blkf[:, half * 8 * CROWS:(half + 1) * 8 * CROWS].rearrange("p (c g n) -> p c g n", c=8, g=4)
                    pe_ = peT[:, v, 8 * half:8 * half + 8].unsqueeze(2).unsqueeze(3).to_broadcast([P, 8, 4, NCMP])
                    ins = dve.tensor_tensor(dst, part, pe_, ALU.add)
                ins.then_inc(sem("blk_sum"), 1)

            def block_lo(v):
                dve.wait_ge(sem("blk_hi"), v + 1)
                dve.tensor_tensor(blk_lo[:].rearrange("p c n -> p (c n)"), blkf,
                                  blk_hi[:].rearrange("p c n -> p (c n)").bitcast(F32), ALU.subtract) \
                    .then_inc(sem("blk_lo"), 1)

            dve.wait_ge(sem("pe_loaded"), 32)
            dve.wait_ge(sem("c2T_k"), T)
            dve.wait_ge(sem("c2T_k_half"), T)
            block_sum(0)
            split_lo(dve, 7, SLOT)
            for t in range(T):
                dve.wait_ge(sem("c_turned"), T + t + 1)
                src = bank[t][:].rearrange("p (g s) -> p g s", g=4)
                dve.tensor_copy(c2T[1][0:HD, :, t * P:(t + 1) * P], src[0:HD])
                skip = 1 if t == 0 else 0
                dve.tensor_copy(c2T[1][HD:P, :, t * P + skip - 1:(t + 1) * P - 1], src[HD:P, :, skip:]) \
                    .then_inc(sem("c2T_v"), 1)
            block_lo(0)
            split_lo(dve, 8, SLOT)
            dve.wait_ge(sem("ksv_out"), 4 * T)
            dve.wait_ge(sem("tables"), 2)
            view = kstage.rearrange("p t (i n) -> p t i n", n=HD)
            rope(chain, view, 8, heads_table(cos, 2 * QUAD, 2), heads_table(sin, 2 * QUAD, 2), [T, 2 * QUAD, 8],
                 sem("ks_roped"))
            dve.wait_ge(sem("c2T_v"), T)
            block_sum(1)
            split_lo(dve, 9, SLOT)
            dve.wait_ge(sem("gates_exp"), T)
            gf = gates.rearrange("p t n -> p (t n)")
            chain.link(dve.tensor_scalar(gf, gf, 1.0, None, ALU.add))
            chain.link(dve.reciprocal(gf, gf))
            split_lo(dve, 10, SLOT)
            block_lo(1)
            dve.wait_ge(sem("padded"), 5)
            for k in range(2, 4):
                dve.wait_ge(sem("k_turned"), k + 1)
                dve.tensor_copy(kT[0:HD, :, k * P:(k + 1) * P],
                                bank[(5, 0)[k - 2]][0:HD, :].rearrange("p (g s) -> p g s", g=QUAD)) \
                    .then_inc(sem("kT_out"), 1)
            split_lo(dve, 11, 3 * KVW)
            split_lo(dve, 12, 3 * KVW)
            split_lo(dve, 13, 2 * KVW)
            rotate("nsa", 0)
            split_lo(dve, NSA_Q1, 3 * KVW)
            dve.wait_ge(sem("kcmp_done"), 1)
            chain.link(dve.tensor_copy(kcs[0:CROWS, :], bank[4][0:CROWS, 0:HD]))
            rope(chain, kcs[0:CROWS, :], 8, cos[0:CROWS, T, 0:16:2], sin[0:CROWS, T, 0:16:2], [8], sem("kcmp_roped"))
            dve.wait_ge(sem("vcmp_done"), 1)
            dve.wait_ge(sem("masks"), 2 * T + 2)
            for g in range(TURNS):
                ins = dve.tensor_tensor(
                    vbd[0:CROWS, g, :].rearrange("p (i n) -> p i n", i=QUAD),
                    bank[7][0:CROWS, g * HD:(g + 1) * HD].unsqueeze(1).to_broadcast([CROWS, QUAD, HD]),
                    blockmask[0:CROWS, :].unsqueeze(2).to_broadcast([CROWS, QUAD, HD]), ALU.mult)
            ins.then_inc(sem("nsa_out"), 1)

            dve.wait_ge(sem("masks"), 2 * T + 2)
            attend("nsa", 0, False, opening=True)
            split_lo(dve, NSA_Q1 + 1, 3 * KVW)
            split_lo(dve, NSA_Q1 + 2, 2 * KVW)
            with dve.Fori(0, TURNS - 2) as turn:
                chain.enter(turn, NSA_LINKS)
                attend("nsa", turn, False, lambda k: split_lo(dve, NSA_Q1 + 3 + k, (3, 3, 2)[k] * KVW, turn))
            chain.leave(TURNS - 2)
            attend("nsa", TURNS - 2, False)
            attend("nsa", TURNS - 1, True)
            output_norm_ffn(0, NSA_OUT, FFN0)
            hidden_lo = ffn(FFN0, 1)
            split_lo(dve, MLA_IN, SLOT)
            hidden_lo(STEPS - 1)

            boundary_dve(chain, 1, FFN0 + 3 * STEPS - 1)
            wait_pool_split(dve, MLA_IN + 1)
            split_lo(dve, MLA_IN + 2, SLOT)
            split_lo(dve, MLA_IN + 3, SLOT)
            dve.wait_ge(sem("lat_gain_loaded"), 16)

            def latents_gained(t, b):
                dve.wait_ge(sem("lat_squared"), 2 * b + t + 1)
                dve.tensor_tensor(lat[:, t, 512 * b:512 * (b + 1)], bank[2 * b + t][:], lat_g[:, 512 * b:512 * (b + 1)],
                                  ALU.mult).then_inc(sem("lat_ready"), 1)

            def latents_lo(t, b):
                dve.wait_ge(sem("lat_hi"), 2 * b + t + 1)
                dve.tensor_tensor(act_part(lat_lo, t, b), lat_bank(t, b)[:].rearrange("p (c n) -> p c n", c=4),
                                  act_part(lat_hi, t, b).bitcast(F32), ALU.subtract).then_inc(sem("lat_lo"), 1)

            for t in range(T):
                latents_gained(t, 0)
            split_lo(dve, MLA_IN + 4, KC * ROPE)
            for t in range(T):
                latents_lo(t, 0)
            for t in range(T):
                latents_gained(t, 1)
            split_lo(dve, MLA_UP0, 3 * QUAD * DK)
            for t in range(T):
                latents_lo(t, 1)
            split_lo(dve, MLA_UP0 + 1, 3 * QUAD * DK)
            for t in range(T):
                for part, width in enumerate((QLAT, KVLAT)):
                    dve.wait_ge(sem("lat_roots"), 2 * t + part + 1)
                    invert(chain, lat_root(t, part), lstats[:, 3 * t + 1 + part:3 * t + 2 + part], width,
                           lstats[:, 10 + t:11 + t] if part == 0 else EPS)
                    dve.tensor_tensor(lat_root(t, part), lat_root(t, part), pre_scale(2, t),
                                      ALU.mult).then_inc(sem("lat_inverted"), 1)
            dve.wait_ge(sem("lat_out"), T)
            rope(chain, lat[:, :, D:D + ROPE], 16, cos[:, 0:T, :], sin[:, 0:T, :], [T, 16])
            for t in range(T):
                ins = dve.tensor_copy(mk[:, t, :, NOPE:],
                                      lat[:, t, D:D + ROPE].unsqueeze(1).to_broadcast([P, QUAD, ROPE]))
            ins.then_inc(sem("mla_out"), 1)
            split_lo(dve, MLA_UP0 + 2, KVC * 512)
            rotate("mla", 0)
            widths = (3 * QUAD * DK, 3 * QUAD * DK, KVC * 512)
            split_lo(dve, MLA_UP1, widths[0])
            keys_out(0)
            attend("mla", 0, False, opening=True)
            split_lo(dve, MLA_UP1 + 1, widths[1])
            split_lo(dve, MLA_UP1 + 2, widths[2])
            with dve.Fori(0, TURNS - 2) as turn:
                chain.enter(turn, MLA_LINKS)
                attend("mla", turn, False, lambda k: split_lo(dve, MLA_UP1 + 3 + k, widths[k], turn))
            chain.leave(TURNS - 2)
            attend("mla", TURNS - 2, False)
            attend("mla", TURNS - 1, True)
            output_norm_ffn(2, MLA_OUT, FFN1)
            hidden_lo = ffn(FFN1, 3)
            hidden_lo(STEPS - 1)
            gained(dve, 3, 0, TILES - 1)
            post_invert(chain, 3, 0)
            gained(dve, 3, 1, TILES - 1)
            post_norm(chain, 3, 0, go_on=False)
            post_invert(chain, 3, 1)
            post_norm(chain, 3, 1, go_on=False)


def kernel(x, positions, ln_mix_pre, ln_mix_post, ln_ffn_pre, ln_ffn_post, ffn_w_gate, ffn_w_up, ffn_w_down,
           nsa_w_in, nsa_cmp_pe_k, nsa_cmp_w1_k, nsa_cmp_w2_k, nsa_cmp_pe_v, nsa_cmp_w1_v, nsa_cmp_w2_v, nsa_w_out,
           mla_w_in, mla_q_norm, mla_kv_norm, mla_w_q_up, mla_w_kv_up, mla_w_out, **unused):
    import numpy as np
    import concourse.bacc as bacc
    from concourse.bass_utils import run_bass_kernel_spmd as run

    def stacked(parts, axis):
        return np.stack([np.asarray(p) for p in parts], axis=axis)

    layers = 2
    pos = np.asarray(positions)[0]
    gate_up = stacked([np.asarray(w).reshape(layers, D, STEPS, FB) for w in (ffn_w_gate, ffn_w_up)], 3)
    arrays = {
        "x": np.asarray(x)[0],
        "positions": stacked([pos[0:P], pos[P:SEQ],
                              np.resize(np.concatenate([pos[CMP_LEN - 1::CMP_STRIDE]] * 4), P)], 1),
        "inv_freq": (np.float32(500000.0) ** (-np.arange(16, dtype=np.float32) / np.float32(16)))
        .astype(np.float32).reshape(1, 16),
        "gains": stacked([ln_mix_pre, ln_mix_post, ln_ffn_pre, ln_ffn_post], 1).reshape(4 * layers, D),
        "lat_gain": np.concatenate([np.asarray(mla_q_norm), np.asarray(mla_kv_norm)], axis=1),
        "nsa_w_in": np.asarray(nsa_w_in)[0],
        "pe_k": np.ascontiguousarray(np.asarray(nsa_cmp_pe_k)[0].reshape(CK, P).T),
        "pe_v": np.ascontiguousarray(np.asarray(nsa_cmp_pe_v)[0].reshape(CK, P).T),
        "w1_k": np.asarray(nsa_cmp_w1_k)[0], "w1_v": np.asarray(nsa_cmp_w1_v)[0],
        "w2_k": np.asarray(nsa_cmp_w2_k)[0], "w2_v": np.asarray(nsa_cmp_w2_v)[0],
        "nsa_w_out": np.asarray(nsa_w_out)[0],
        "mla_w_in": np.asarray(mla_w_in)[0], "w_q_up": np.asarray(mla_w_q_up)[0],
        "w_kv_up": np.asarray(mla_w_kv_up)[0], "mla_w_out": np.asarray(mla_w_out)[0],
        "w_gate_up": gate_up.reshape(layers, D, 2 * F),
        "w_down": np.asarray(ffn_w_down),
    }
    arrays = {name: np.ascontiguousarray(a) for name, a in arrays.items()}
    nc = bacc.Bacc("TRN2", target_bir_lowering=False, num_devices=1)
    args = {name: nc.dram_tensor(f"in_{name}", a.shape, mybir.dt.from_np(a.dtype), kind="ExternalInput").ap()
            for name, a in arrays.items()}
    out = nc.dram_tensor("out", (SEQ, D), F32, kind="ExternalOutput").ap()
    trunk(nc, out=out, **args)
    result = run(nc, [{f"in_{name}": a for name, a in arrays.items()}], core_ids=[0])
    return result.results[0]["out"].reshape(1, SEQ, D)
```
